# Optimizing a Trainium2 kernel written in Bass

```python
import jax, jax.numpy as jnp
from jax import lax
import numpy as np

D_MODEL = 1024
BATCH = 1
SEQ = 256
DEPTH = 1

HEAD_DIM = 64
N_FOX_HEADS = 8
N_MOBA_HEADS = 8
FOX_WIDTH = N_FOX_HEADS * HEAD_DIM
MOBA_WIDTH = N_MOBA_HEADS * HEAD_DIM
MIX_WIDTH = FOX_WIDTH + MOBA_WIDTH
IN_COLS = 3 * FOX_WIDTH + N_FOX_HEADS + 3 * MOBA_WIDTH
FOX_Q_BLOCK = 128
MOBA_BLOCK = 256
MOBA_TOPK = 3
MOBA_Q_CHUNK = 16
ROPE_THETA = 500000.0
ROPE_DIM = HEAD_DIM // 4
N_GROUPS = 4
EXPERTS_PER_GROUP = 8
N_EXPERTS = N_GROUPS * EXPERTS_PER_GROUP
TOPK_IN_GROUP = 2
D_EXPERT = 256
EPS = 1e-6
F32 = jnp.float32

kernel_name = "hymba_fox_moba_hmoe_layer"

def rms_norm(x, g):
    xf = x.astype(F32)
    y = xf * lax.rsqrt(jnp.mean(xf * xf, axis=-1, keepdims=True) + EPS)
    return (y * g.astype(F32)).astype(x.dtype)

def to_heads(t, n_heads):
    b, s, _ = t.shape
    return t.reshape(b, s, n_heads, HEAD_DIM).transpose(0, 2, 1, 3)

def from_heads(t):
    b, h, s, d = t.shape
    return t.transpose(0, 2, 1, 3).reshape(b, s, h * d)

def partial_rotary(t):
    seq = t.shape[2]
    half = ROPE_DIM // 2
    inv_freq = ROPE_THETA ** (-jnp.arange(half, dtype=F32) / half)
    ang = jnp.arange(seq, dtype=F32)[:, None] * inv_freq[None, :]
    cos, sin = jnp.cos(ang), jnp.sin(ang)
    tr = t[..., :ROPE_DIM].astype(F32)
    t1, t2 = tr[..., :half], tr[..., half:]
    rot = jnp.concatenate([t1 * cos - t2 * sin, t2 * cos + t1 * sin], axis=-1).astype(t.dtype)
    return jnp.concatenate([rot, t[..., ROPE_DIM:]], axis=-1)

def forgetting_attention(q, k, v, log_f):
    b, h, s, d = q.shape
    nb = s // FOX_Q_BLOCK
    c = jnp.cumsum(log_f, axis=-1)
    q_blocks = q.reshape(b, h, nb, FOX_Q_BLOCK, d).transpose(2, 0, 1, 3, 4)
    c_blocks = c.reshape(b, h, nb, FOX_Q_BLOCK).transpose(2, 0, 1, 3)
    key_pos = jnp.arange(s)
    scale = HEAD_DIM ** -0.5

    def one_block(args):
        i, qb, cb = args
        sc = jnp.einsum('bhqd,bhkd->bhqk', qb, k, preferred_element_type=F32) * scale
        sc = sc + cb[..., :, None] - c[:, :, None, :]
        q_pos = i * FOX_Q_BLOCK + jnp.arange(FOX_Q_BLOCK)
        sc = jnp.where(key_pos[None, :] <= q_pos[:, None], sc, -jnp.inf)
        p = jax.nn.softmax(sc, axis=-1)
        return jnp.einsum('bhqk,bhkd->bhqd', p.astype(v.dtype), v)

    out = lax.map(one_block, (jnp.arange(nb), q_blocks, c_blocks))
    return out.transpose(1, 2, 0, 3, 4).reshape(b, h, s, d)

def moba_attention(q, k, v):
    b, h, s, d = q.shape
    nblk = -(-s // MOBA_BLOCK)
    pad = nblk * MOBA_BLOCK - s
    k_blk = jnp.pad(k, ((0, 0), (0, 0), (0, pad), (0, 0))).reshape(b, h, nblk, MOBA_BLOCK, d)
    v_blk = jnp.pad(v, ((0, 0), (0, 0), (0, pad), (0, 0))).reshape(b, h, nblk, MOBA_BLOCK, d)
    k_mean = jnp.mean(k_blk.astype(F32), axis=3)
    topk = min(MOBA_TOPK, nblk)
    nq = s // MOBA_Q_CHUNK
    q_chunks = q.reshape(b, h, nq, MOBA_Q_CHUNK, d).transpose(2, 0, 1, 3, 4)
    b_idx = jnp.arange(b)[:, None, None, None]
    h_idx = jnp.arange(h)[None, :, None, None]
    blk_ids = jnp.arange(nblk)
    scale = HEAD_DIM ** -0.5

    def one_chunk(args):
        i, qc = args
        q_pos = i * MOBA_Q_CHUNK + jnp.arange(MOBA_Q_CHUNK)
        own = q_pos[0] // MOBA_BLOCK
        gate = jnp.einsum('bhqd,bhnd->bhqn', qc.astype(F32), k_mean)
        gate = jnp.where(blk_ids < own, gate, -jnp.inf)
        _, sel = lax.top_k(gate, topk)
        sel_valid = sel < own
        k_sel = k_blk[b_idx, h_idx, sel]
        v_sel = v_blk[b_idx, h_idx, sel]
        s_sel = jnp.einsum('bhqd,bhqjkd->bhqjk', qc, k_sel, preferred_element_type=F32) * scale
        s_sel = jnp.where(sel_valid[..., None], s_sel, -jnp.inf)
        s_sel = s_sel.reshape(b, h, MOBA_Q_CHUNK, topk * MOBA_BLOCK)
        k_own = lax.dynamic_index_in_dim(k_blk, own, axis=2, keepdims=False)
        v_own = lax.dynamic_index_in_dim(v_blk, own, axis=2, keepdims=False)
        own_pos = own * MOBA_BLOCK + jnp.arange(MOBA_BLOCK)
        s_own = jnp.einsum('bhqd,bhkd->bhqk', qc, k_own, preferred_element_type=F32) * scale
        s_own = jnp.where(own_pos[None, :] <= q_pos[:, None], s_own, -jnp.inf)
        p = jax.nn.softmax(jnp.concatenate([s_sel, s_own], axis=-1), axis=-1)
        p_sel = p[..., :topk * MOBA_BLOCK].reshape(b, h, MOBA_Q_CHUNK, topk, MOBA_BLOCK)
        p_own = p[..., topk * MOBA_BLOCK:]
        return (jnp.einsum('bhqjk,bhqjkd->bhqd', p_sel.astype(v.dtype), v_sel)
                + jnp.einsum('bhqk,bhkd->bhqd', p_own.astype(v.dtype), v_own))

    out = lax.map(one_chunk, (jnp.arange(nq), q_chunks))
    return out.transpose(1, 2, 0, 3, 4).reshape(b, h, s, d)

def hierarchical_moe(h, w_rg, b_rg, w_re, b_re, w_gate, w_up, w_down):
    g_prob = jax.nn.softmax(jnp.einsum('bsd,dg->bsg', h, w_rg, preferred_element_type=F32)
                            + b_rg.astype(F32), axis=-1)
    g_top, g_idx = lax.top_k(g_prob, 1)
    e_logits = jnp.einsum('bsd,dge->bsge', h, w_re, preferred_element_type=F32) + b_re.astype(F32)
    e_logits = jnp.take_along_axis(e_logits, g_idx[..., None], axis=2)[..., 0, :]
    e_prob = jax.nn.softmax(e_logits, axis=-1)
    e_top, e_idx = lax.top_k(e_prob, TOPK_IN_GROUP)
    e_w = e_top / jnp.sum(e_top, axis=-1, keepdims=True) * g_top
    flat_idx = g_idx * EXPERTS_PER_GROUP + e_idx
    combine = jnp.sum(jax.nn.one_hot(flat_idx, N_EXPERTS, dtype=F32) * e_w[..., None], axis=-2)

    def per_sequence(args):
        hs, cs = args
        a = jnp.einsum('sd,edf->sef', hs, w_gate)
        u = jnp.einsum('sd,edf->sef', hs, w_up)
        act = jax.nn.silu(a) * u * cs[..., None].astype(hs.dtype)
        return jnp.einsum('sef,efd->sd', act, w_down)

    return lax.map(per_sequence, (h, combine))

def setup_inputs(seed: int = 0) -> dict:
    key = jax.random.key(seed)
    ks = jax.random.split(key, 16)
    nrm = jax.random.normal
    return {
        "x": nrm(ks[0], (BATCH, SEQ, D_MODEL), F32),
        "norm_mix_g": 1.0 + 0.02 * nrm(ks[1], (DEPTH, D_MODEL), F32),
        "w_in": nrm(ks[2], (DEPTH, D_MODEL, IN_COLS), F32) * D_MODEL ** -0.5,
        "b_forget": 3.0 + 0.5 * nrm(ks[3], (DEPTH, N_FOX_HEADS), F32),
        "fox_out_g": 1.0 + 0.02 * nrm(ks[4], (DEPTH, FOX_WIDTH), F32),
        "moba_out_g": 1.0 + 0.02 * nrm(ks[5], (DEPTH, MOBA_WIDTH), F32),
        "w_out": nrm(ks[6], (DEPTH, MIX_WIDTH, D_MODEL), F32) * MIX_WIDTH ** -0.5,
        "norm_ffn_g": 1.0 + 0.02 * nrm(ks[7], (DEPTH, D_MODEL), F32),
        "w_router_group": nrm(ks[8], (DEPTH, D_MODEL, N_GROUPS), F32) * D_MODEL ** -0.5,
        "b_router_group": 0.01 * nrm(ks[9], (DEPTH, N_GROUPS), F32),
        "w_router_expert": nrm(ks[10], (DEPTH, D_MODEL, N_GROUPS, EXPERTS_PER_GROUP), F32) * D_MODEL ** -0.5,
        "b_router_expert": 0.01 * nrm(ks[11], (DEPTH, N_GROUPS, EXPERTS_PER_GROUP), F32),
        "w_gate": nrm(ks[12], (DEPTH, N_EXPERTS, D_MODEL, D_EXPERT), F32) * D_MODEL ** -0.5,
        "w_up": nrm(ks[13], (DEPTH, N_EXPERTS, D_MODEL, D_EXPERT), F32) * D_MODEL ** -0.5,
        "w_down": nrm(ks[14], (DEPTH, N_EXPERTS, D_EXPERT, D_MODEL), F32) * D_EXPERT ** -0.5,
        "norm_final_g": 1.0 + 0.02 * nrm(ks[15], (D_MODEL,), F32),
    }

def reference(x, norm_mix_g, w_in, b_forget, fox_out_g, moba_out_g, w_out, norm_ffn_g,
              w_router_group, b_router_group, w_router_expert, b_router_expert,
              w_gate, w_up, w_down, norm_final_g):
    splits = [FOX_WIDTH, 2 * FOX_WIDTH, 3 * FOX_WIDTH, 3 * FOX_WIDTH + N_FOX_HEADS,
              3 * FOX_WIDTH + N_FOX_HEADS + MOBA_WIDTH,
              3 * FOX_WIDTH + N_FOX_HEADS + 2 * MOBA_WIDTH]
    for l in range(DEPTH):
        h = rms_norm(x, norm_mix_g[l])
        proj = jnp.einsum('bsd,dc->bsc', h, w_in[l])
        fq, fk, fv, f_logit, mq, mk, mv = jnp.split(proj, splits, axis=-1)
        log_f = jax.nn.log_sigmoid(f_logit.astype(F32) + b_forget[l].astype(F32)).transpose(0, 2, 1)
        fox = forgetting_attention(to_heads(fq, N_FOX_HEADS), to_heads(fk, N_FOX_HEADS),
                                   to_heads(fv, N_FOX_HEADS), log_f)
        moba = moba_attention(partial_rotary(to_heads(mq, N_MOBA_HEADS)),
                              partial_rotary(to_heads(mk, N_MOBA_HEADS)),
                              to_heads(mv, N_MOBA_HEADS))
        mixed = jnp.concatenate([rms_norm(from_heads(fox), fox_out_g[l]),
                                 rms_norm(from_heads(moba), moba_out_g[l])], axis=-1)
        x = x + jnp.einsum('bsc,cd->bsd', mixed, w_out[l])
        h = rms_norm(x, norm_ffn_g[l])
        x = x + hierarchical_moe(h, w_router_group[l], b_router_group[l], w_router_expert[l],
                                 b_router_expert[l], w_gate[l], w_up[l], w_down[l])
    return rms_norm(x, norm_final_g)


_drawn_inputs = setup_inputs


def setup_inputs(seed=0):
    import zlib

    import numpy as np

    out = dict(_drawn_inputs(seed))
    spreads = {}
    factors = {'fox_out_g': 12.058,
     'moba_out_g': 10.714,
     'b_router_group': 38.0,
     'b_router_expert': 20.671,
     'norm_final_g': 8.261,
     'norm_ffn_g': 5.308}
    for name, (base, spread) in spreads.items():
        noise = np.random.default_rng([zlib.crc32(name.encode()), seed]).standard_normal(out[name].shape)
        drawn = base * np.exp(spread * noise) if base else spread * noise
        out[name] = __import__('jax').numpy.asarray(drawn.astype(out[name].dtype))
    for name, factor in factors.items():
        out[name] = (out[name] * factor).astype(out[name].dtype)
    return out
```

```python
import concourse.bass as bass
from concourse import mybir
from contextlib import ExitStack

P = 128
SEQ = 256
D = 1024
HD = 64
NT = SEQ // P
KD = D // P
FOX_W = 512
MOBA_W = 512
N_FOX = FOX_W // HD
N_MOBA = MOBA_W // HD
MIX_W = FOX_W + MOBA_W
PAIRS = MIX_W // P
FOX_PAIRS = FOX_W // P
ROT = HD // 8
N_GROUPS = 4
EPG = 8
E = N_GROUPS * EPG
FE = 256
EPS = 1e-6
SCALE = HD ** -0.5
HALF = 512
CAP = 64
ROUNDS_MAX = SEQ // CAP
NSLOT = 6
SLOT = 3 * KD * FE
LOOPS = E // NSLOT
TAIL = E - LOOPS * NSLOT
LG = 8 + E
NEG = -3.0e38
C_ID, C_IOTA, C_COS, C_SIN, C_END = 0, P, 2 * P, 2 * P + NT * ROT, 2 * P + 2 * NT * ROT


def layer_program(nc, I, out):
    fp32, bf16 = mybir.dt.float32, mybir.dt.bfloat16
    i32, u32 = mybir.dt.int32, mybir.dt.uint32
    ALU, ACT, AX = mybir.AluOpType, mybir.ActivationFunctionType, mybir.AxisListType.X
    ctx = ExitStack()
    with ctx:
        def sb(name, shape, dt=fp32):
            return ctx.enter_context(nc.sbuf_tensor(name, shape, dt))

        def sem(name):
            return ctx.enter_context(nc.semaphore(name))

        ring = sb("ring", [P, NSLOT * SLOT])
        x = sb("x", [P, NT, D])
        hT = sb("hT", [P, KD, SEQ])
        qk = sb("qk", [P, 2 * PAIRS, SEQ])
        v = sb("v", [P, NT, MIX_W])
        stage = sb("stage", [P, NT * D])
        pp = sb("pp", [P, 3072])
        cf = sb("cf", [P, C_END])
        cb = sb("cb", [P, 4 * P], bf16)
        gcol = sb("gcol", [P, 2 * KD])
        wr = sb("wr", [P, KD, LG])
        stats = sb("stats", [P, 40])

        ident, iota = cf[:, C_ID:C_ID + P], cf[:, C_IOTA:C_IOTA + P]
        identb, causal = cb[:, 0:P], cb[:, P:2 * P]
        before, onesb = cb[:, 2 * P:3 * P], cb[:, 3 * P:4 * P]
        qT, kT = qk[:, 0:PAIRS, :], qk[:, PAIRS:2 * PAIRS, :]
        oT = qT
        xn = stage[:, :].rearrange("p (t d) -> p t d", t=NT)
        mqk = stage[:, :].rearrange("p (w t c) -> p w t c", w=2, t=NT)
        WI = KD * FOX_W
        w_blk = [ring[:, b * WI:(b + 1) * WI].rearrange("p (k c) -> p k c", k=KD) for b in range(6)]
        WO = 6 * WI
        w_o = ring[:, WO:WO + KD * D].rearrange("p (k c) -> p k c", k=KD)
        T0 = WO + KD * D
        wf = ring[:, T0:T0 + KD * N_FOX].rearrange("p (k c) -> p k c", k=KD)
        gvec = ring[0:2 * KD, T0 + 64:T0 + 64 + P]
        neg8 = ring[0:N_FOX, T0 + 192:T0 + 192 + N_FOX * P].rearrange("p (h c) -> p h c", h=N_FOX)
        ropet = ring[:, T0 + 1216:T0 + 1216 + 4 * N_MOBA * ROT].rearrange("p (i h r) -> p i h r", i=4, h=N_MOBA)
        sqt = ring[:, T0 + 1472:T0 + 1472 + SEQ]
        sqacc = ring[:, T0 + 1728:T0 + 1728 + 2 * SEQ].rearrange("p (g t) -> p g t", g=2)
        bfg = ring[0:N_FOX, T0 + 2240:T0 + 2241]
        fz, fa = v[0:N_FOX, 0, FOX_W:FOX_W + SEQ], v[0:N_FOX, 0, FOX_W + SEQ:MIX_W]
        fc, fl = v[0:N_FOX, 1, FOX_W:FOX_W + SEQ], v[0:N_FOX, 1, FOX_W + SEQ:MIX_W]
        PW = P + SEQ
        prob = [[pp[:, (2 * s + h) * PW:(2 * s + h + 1) * PW] for h in range(2)] for s in range(2)]
        probT = [[pp[:, (4 + 2 * s + h) * PW:(5 + 2 * s + h) * PW] for h in range(2)] for s in range(2)]
        ssq, var, seed, rstd, rt = (stats[:, 2 * i:2 * i + 2] for i in range(5))
        mx = [stats[:, 10 + 4 * s:14 + 4 * s] for s in range(2)]
        nm = [stats[:, 18 + 4 * s:22 + 4 * s] for s in range(2)]
        rs = [stats[:, 26 + 4 * s:30 + 4 * s] for s in range(2)]
        onescol = stats[:, 34:35]
        h2 = v
        h2T = hT
        res = pp[:, 0:NT * D].rearrange("p (t k c) -> p t k c", t=NT, k=KD)
        qkf = qk[:, :, :].rearrange("p a b -> p (a b)")
        hs = qkf[:, 0:3 * D].bitcast(bf16).rearrange("p (i t k c) -> p i t k c", i=3, t=NT, k=KD)
        gffn, gfin = stage[:, 0:D], stage[:, D:2 * D]
        rtr = qkf[:, 3 * D:4 * D]
        cur = [0]

        def take(n, dt=fp32):
            cur[0] += n
            got = rtr[:, cur[0] - n:cur[0]]
            return got if dt is fp32 else got.bitcast(dt)

        lg = take(NT * LG).rearrange("p (t c) -> p t c", t=NT)
        biasb = take(LG)
        rank = take(NT * E).rearrange("p (t e) -> p t e", t=NT)
        wgt = take(NT * E).rearrange("p (t e) -> p t e", t=NT)
        member = take(NT * E // 2, bf16).rearrange("p (t e) -> p t e", t=NT)
        memf = take(NT * E).rearrange("p (t e) -> p t e", t=NT)
        wa, wb = take(E), take(E)
        top8 = take(NT * 8).rearrange("p (t c) -> p t c", t=NT)
        idx8 = take(NT * 8, u32).rearrange("p (t c) -> p t c", t=NT)
        etop8 = take(NT * 8).rearrange("p (t c) -> p t c", t=NT)
        eidx8 = take(NT * 8, u32).rearrange("p (t c) -> p t c", t=NT)
        el8 = take(NT * 8).rearrange("p (t c) -> p t c", t=NT)
        gexp = take(NT * 8).rearrange("p (t c) -> p t c", t=NT)
        gmask = take(NT * N_GROUPS).rearrange("p (t c) -> p t c", t=NT)
        one = [[take(1) for _ in range(10)] for _ in range(NT)]
        most, nrounds = take(1), take(1)
        rounds_i = take(1, i32)
        ttot = take(1)
        hTf = hT[:, :, :].rearrange("p a b -> p (a b)")
        hg = hTf[:, 0:HALF].rearrange("p (k c) -> p k c", k=KD)
        yb = [hTf[:, HALF * (1 + i):HALF * (2 + i)] for i in range(2)]
        selT = [hTf[:, 3 * HALF + SEQ * i:3 * HALF + SEQ * (i + 1)] for i in range(2)]
        M0 = NT * D
        selw = pp[:, M0:M0 + NT * P].rearrange("p (t c) -> p t c", t=NT)
        selb = pp[:, M0 + 256:M0 + 320].bitcast(bf16).rearrange("p (t c) -> p t c", t=NT)
        act_sb = pp[:, M0 + 320:M0 + 448]
        sig, gated = pp[:, M0 + 448:M0 + 576], pp[:, M0 + 576:M0 + 704]
        actT = pp[:, M0 + 704:M0 + 832]
        slot = [ring[:, s * SLOT:(s + 1) * SLOT] for s in range(NSLOT)]
        s_gu = [s[:, 0:2 * KD * FE].rearrange("p (w k h f) -> p w k h f", w=2, k=KD, h=2) for s in slot]
        s_dn = [s[:, 2 * KD * FE:].rearrange("p (h n) -> p h n", h=2) for s in slot]
        outb = [x[:, t, :] for t in range(NT)]

        bank = [ctx.enter_context(nc.psum_tensor(f"bank{i}", [P, HALF], fp32)) for i in range(8)]
        O_BANK = 3
        acc = [[bank[0], bank[1]], [bank[2], bank[3]]]
        p_hg, p_gu, p_tr, p_y = bank[4], bank[5], bank[6], bank[7]

        x_in, cst_in, wf_in, wo_in, gv_in, wr_in = (sem(n) for n in ("x_in", "cst_in", "wf_in", "wo_in", "gv_in", "wr_in"))
        gains_in = sem("gains_in")
        blk_in = [sem(f"blk_in{b}") for b in range(6)]
        slot_in = [sem(f"slot_in{s}") for s in range(NSLOT)]
        out_done = sem("out_done")
        pool_step, dve_step, act_step = sem("pool_step"), sem("dve_step"), sem("act_step")
        ones_set, gcol_t, gcol_set = sem("ones_set"), sem("gcol_t"), sem("gcol_set")
        ssq_ready, var_ready, seed_ready, xn_ready = (sem(n) for n in ("ssq_ready", "var_ready", "seed_ready", "xn_ready"))
        tr_done, hT_act, hT_dve = sem("tr_done"), sem("hT_act"), sem("hT_dve")
        grp_done, act_took, dve_took = sem("grp_done"), sem("act_took"), sem("dve_took")
        fz_ready, fa_ready, fl_ready, fc_ready = (sem(n) for n in ("fz_ready", "fa_ready", "fl_ready", "fc_ready"))
        s_done, nm_ready, exp_done, p_ready, t_done = (sem(n) for n in ("s_done", "nm_ready", "exp_done", "p_ready", "t_done"))
        pt_act, pt_dve, o_done, o_taken, o_ready = (sem(n) for n in ("pt_act", "pt_dve", "o_done", "o_taken", "o_ready"))
        rope_done, xt_done, xt_act, xt_dve = (sem(n) for n in ("rope_done", "xt_done", "xt_act", "xt_dve"))
        x1_ready, h2_ready, h2t_done = sem("x1_ready"), sem("h2_ready"), sem("h2t_done")
        h2T_act, h2T_dve, logits_done = sem("h2T_act"), sem("h2T_dve"), sem("logits_done")
        gm_ready, gexp_done, ed_ready, eexp_done = (sem(n) for n in ("gm_ready", "gexp_done", "ed_ready", "eexp_done"))
        member_ready, rank_done, rounds_ready = sem("member_ready"), sem("rank_done"), sem("rounds_ready")
        hi_ready, r1_ready, mid_ready, split_ready = (sem(n) for n in ("hi_ready", "r1_ready", "mid_ready", "split_ready"))
        hg_ready, gu_done, sig_ready, sel_ready = (sem(n) for n in ("hg_ready", "gu_done", "sig_ready", "sel_ready"))
        gathered, selT_ready, act_ready, actt_done = (sem(n) for n in ("gathered", "selT_ready", "act_ready", "actt_done"))
        actT_ready, down_done, y_ready, added = (sem(n) for n in ("actT_ready", "down_done", "y_ready", "added"))
        acc_done, fin_ready = sem("acc_done"), sem("fin_ready")

        G_FT, G_FQK, G_FV, G_MQ, G_MK, G_MV = 0, 1, 5, 7, 9, 11
        G_SF, G_OF, G_SM, G_OM = 13, 14, 18, 19

        def grp_bank(g):
            return bank[g % 3]

        def wait_bank_free(pe, g):
            if g >= 3:
                if g - 3 < G_SF:
                    pe.wait_ge(act_took, g - 2)
                else:
                    pe.wait_ge(dve_took, g - 3 - G_SF + 1)

        def pair_heads(j):
            return (2 * j, 2 * j + 1)

        block = ctx.enter_context(nc.Block())

        @block.sync
        def _(sp):
            for t in range(NT):
                sp.dma_start(x[:, t, :], I["x"][0, t * P:(t + 1) * P, :]).then_inc(x_in, 16)
            sp.dma_start(wf, I["w_in"][0, :, 3 * FOX_W:3 * FOX_W + N_FOX].rearrange("(k p) c -> p k c", p=P)).then_inc(wf_in, 16)
            for b in range(6):
                c0 = b * FOX_W + (N_FOX if b >= 3 else 0)
                sp.dma_start(w_blk[b], I["w_in"][0, :, c0:c0 + FOX_W].rearrange("(k p) c -> p k c", p=P)).then_inc(blk_in[b], 16)
            sp.dma_start(w_o, I["w_out"][0].rearrange("(k p) n -> p k n", p=P)).then_inc(wo_in, 16)

            def load(e, s):
                gu = slot[s][:, 0:2 * KD * FE].rearrange("p (w c) -> p w c", w=2)
                sp.dma_start(gu[:, 0, :], I["w_gate"][0, e].rearrange("(p k) f -> p (k f)", p=P) if isinstance(e, int)
                             else I["w_gate"][0, bass.ds(e, 1)].rearrange("o (p k) f -> p (o k f)", p=P)).then_inc(slot_in[s], 16)
                sp.dma_start(gu[:, 1, :], I["w_up"][0, e].rearrange("(p k) f -> p (k f)", p=P) if isinstance(e, int)
                             else I["w_up"][0, bass.ds(e, 1)].rearrange("o (p k) f -> p (o k f)", p=P)).then_inc(slot_in[s], 16)
                sp.dma_start(s_dn[s], I["w_down"][0, e].rearrange("(h p) n -> p h n", p=P) if isinstance(e, int)
                             else I["w_down"][0, bass.ds(e, 1)].rearrange("o (h p) n -> p (o h) n", p=P)).then_inc(slot_in[s], 16)

            for s in range(NSLOT):
                if s == 0:
                    sp.wait_ge(grp_done, G_FQK + 4)
                elif s == 1:
                    sp.wait_ge(grp_done, G_FV + 2)
                elif s == 2:
                    sp.wait_ge(grp_done, G_MK + 2)
                elif s == 3:
                    sp.wait_ge(grp_done, G_MV + 2)
                elif s == 4:
                    sp.wait_ge(grp_done, G_OM + 4)
                    sp.wait_ge(o_ready, PAIRS)
                load(s, s)
            with sp.Fori(1, LOOPS) as g:
                for s in range(NSLOT):
                    sp.wait_ge(down_done, g * NSLOT + (s - NSLOT + 1))
                    load(g * NSLOT + s, s)
            for s in range(TAIL):
                sp.wait_ge(down_done, LOOPS * NSLOT + s - NSLOT + 1)
                load(LOOPS * NSLOT + s, s)
            sp.wait_ge(rounds_ready, 1)
            rounds = sp.value_load(rounds_i[0:1, 0:1], min_val=1, max_val=ROUNDS_MAX)
            with sp.If(rounds > 1):
                with sp.Fori(1, rounds) as r:
                    sp.wait_ge(down_done, r * E)
                    for s in range(NSLOT):
                        load(s, s)
                    with sp.Fori(1, LOOPS) as g:
                        for s in range(NSLOT):
                            sp.wait_ge(down_done, r * E + g * NSLOT + (s - NSLOT + 1))
                            load(g * NSLOT + s, s)
                    for s in range(TAIL):
                        sp.wait_ge(down_done, r * E + (LOOPS * NSLOT + s - NSLOT + 1))
                        load(LOOPS * NSLOT + s, s)
            for t in range(NT):
                sp.wait_ge(fin_ready, t + 1)
                sp.dma_start(out[0, t * P:(t + 1) * P, :], outb[t]).then_inc(out_done, 16)
            sp.wait_ge(out_done, 16 * NT)

        @block.tensor
        def _(pe):
            mm = nc.tensor.matmul
            pe.wait_ge(cst_in, 48)
            pe.wait_ge(gv_in, 64)
            nc.tensor.transpose(bank[0][:, 0:2 * KD], gvec, ident[0:2 * KD, 0:2 * KD]).then_inc(gcol_t, 1)
            for i in range(KD // 2):
                for t in range(NT):
                    pe.wait_ge(xn_ready, t + 1)
                    for k in (2 * i, 2 * i + 1):
                        c = (k % 2) * SEQ + t * P
                        last = nc.tensor.transpose(bank[4 + i][:, c:c + P], xn[:, t, k * P:(k + 1) * P], ident)
                last.then_inc(tr_done, 1)
            pe.wait_ge(hT_act, 1)
            pe.wait_ge(hT_dve, 1)

            def proj_major(g, w, col, width, out_cols):
                for k in range(KD):
                    last = mm(grp_bank(g)[0:width, out_cols:out_cols + SEQ], w[:, k, col:col + width], hT[:, k, :],
                              start=(k == 0), stop=(k == KD - 1))
                return last

            def proj_tokens(g, w, t):
                wait_bank_free(pe, g)
                for k in range(KD):
                    last = mm(grp_bank(g)[:, :], hT[:, k, t * P:(t + 1) * P], w[:, k, :], start=(k == 0), stop=(k == KD - 1))
                last.then_inc(grp_done, 1)

            def scores(j):
                banks = [bank[4 + 2 * (j % 2) + h] for h in range(2)]
                if j >= 2:
                    pe.wait_ge(pt_act, j - 1)
                    pe.wait_ge(pt_dve, j - 1)
                for t in range(NT):
                    nk = (t + 1) * P
                    c = t * P
                    for h in range(2):
                        mm(banks[h][:, c:c + nk], qT[HD * h:HD * (h + 1), j, t * P:(t + 1) * P],
                           kT[HD * h:HD * (h + 1), j, 0:nk], start=True, stop=False)
                    if j < FOX_PAIRS:
                        for h in range(2):
                            mm(banks[h][:, c:c + nk], neg8[:, 2 * j + h, :], fc[:, 0:nk], start=False, stop=False)
                    for h in range(2):
                        last = mm(banks[h][:, c + t * P:c + nk], identb, causal, start=False, stop=True)
                last.then_inc(s_done, 1)

            def transposes(j):
                pe.wait_ge(p_ready, j + 1)
                for h in range(2):
                    b, p = bank[4 + 2 * (j % 2) + h], prob[j % 2][h]
                    for i in range(3):
                        last = nc.tensor.transpose(b[:, i * P:(i + 1) * P], p[:, i * P:(i + 1) * P], ident)
                last.then_inc(t_done, 1)

            def values(j):
                pe.wait_ge(pt_act, j + 1)
                pe.wait_ge(pt_dve, j + 1)
                if j >= 1:
                    pe.wait_ge(o_taken, j)
                for h in range(2):
                    mm(bank[O_BANK][HD * h:HD * (h + 1), 0:SEQ], v[:, 0, HD * (2 * j + h):HD * (2 * j + h + 1)],
                       probT[j % 2][h][:, 0:SEQ], start=True, stop=False)
                for h in range(2):
                    last = mm(bank[O_BANK][HD * h:HD * (h + 1), P:SEQ], v[:, 1, HD * (2 * j + h):HD * (2 * j + h + 1)],
                              probT[j % 2][h][:, SEQ:PW], start=False, stop=True)
                last.then_inc(o_done, 1)

            def sum_squares(g, group):
                wait_bank_free(pe, g)
                pe.wait_ge(o_ready, FOX_PAIRS * (group + 1))
                for t in range(NT):
                    last = mm(grp_bank(g)[:, t:t + 1], sqacc[:, group, t * P:(t + 1) * P], onescol, start=True, stop=True)
                last.then_inc(grp_done, 1)

            def out_proj(g, group, t, half):
                wait_bank_free(pe, g)
                for k in range(FOX_PAIRS):
                    j = FOX_PAIRS * group + k
                    last = mm(grp_bank(g)[:, :], oT[:, j, t * P:(t + 1) * P], w_o[:, j, half * HALF:(half + 1) * HALF],
                              start=(k == 0), stop=(k == FOX_PAIRS - 1))
                last.then_inc(grp_done, 1)

            pe.wait_ge(wf_in, 16)
            pe.wait_ge(gcol_set, 1)
            proj_major(G_FT, wf, 0, N_FOX, 0).then_inc(grp_done, 1)
            for w in range(2):
                pe.wait_ge(blk_in[w], 16)
                for i in range(2):
                    g = G_FQK + 2 * w + i
                    wait_bank_free(pe, g)
                    proj_major(g, w_blk[w], (2 * i) * P, P, 0)
                    proj_major(g, w_blk[w], (2 * i + 1) * P, P, SEQ).then_inc(grp_done, 1)
            pe.wait_ge(blk_in[2], 16)
            for t in range(NT):
                proj_tokens(G_FV + t, w_blk[2], t)
            pe.wait_ge(act_took, G_FV)
            pe.wait_ge(fc_ready, 1)
            pe.wait_ge(gv_in, 64)
            scores(0)
            scores(1)
            pe.wait_ge(blk_in[3], 16)
            proj_tokens(G_MQ, w_blk[3], 0)
            pe.wait_ge(act_took, G_MQ)
            transposes(0)
            transposes(1)
            proj_tokens(G_MQ + 1, w_blk[3], 1)
            values(0)
            scores(2)
            values(1)
            scores(3)
            pe.wait_ge(blk_in[4], 16)
            proj_tokens(G_MK, w_blk[4], 0)
            transposes(2)
            transposes(3)
            proj_tokens(G_MK + 1, w_blk[4], 1)
            values(2)
            values(3)
            pe.wait_ge(blk_in[5], 16)
            proj_tokens(G_MV, w_blk[5], 0)
            pe.wait_ge(rope_done, 4)
            for w in range(2):
                for i in range(FOX_PAIRS):
                    for t in range(NT):
                        c = (i % 2) * SEQ + t * P
                        last = nc.tensor.transpose(bank[4 + 2 * w + i // 2][:, c:c + P], mqk[:, w, t, i * P:(i + 1) * P], ident)
            last.then_inc(xt_done, 1)
            proj_tokens(G_MV + 1, w_blk[5], 1)
            pe.wait_ge(xt_act, 1)
            pe.wait_ge(xt_dve, 1)
            scores(4)
            scores(5)
            sum_squares(G_SF, 0)
            pe.wait_ge(wo_in, 16)
            out_proj(G_OF, 0, 0, 0)
            out_proj(G_OF + 1, 0, 0, 1)
            transposes(4)
            transposes(5)
            out_proj(G_OF + 2, 0, 1, 0)
            pe.wait_ge(act_took, G_SF)
            values(4)
            scores(6)
            values(5)
            scores(7)
            out_proj(G_OF + 3, 0, 1, 1)
            transposes(6)
            transposes(7)
            values(6)
            values(7)
            sum_squares(G_SM, 1)
            for i in range(4):
                out_proj(G_OM + i, 1, i // 2, i % 2)

            for i in range(KD // 2):
                for t in range(NT):
                    pe.wait_ge(h2_ready, t + 1)
                    for k in (2 * i, 2 * i + 1):
                        c = (k % 2) * SEQ + t * P
                        last = nc.tensor.transpose(bank[4 + i][:, c:c + P], h2[:, t, k * P:(k + 1) * P], ident)
                last.then_inc(h2t_done, 1)
            pe.wait_ge(dve_took, G_OM + 4 - G_SF)
            for t in range(NT):
                for half in range(2):
                    mm(acc[t][half][:, :], ident, x[:, t, half * HALF:(half + 1) * HALF], start=True, stop=False)
            pe.wait_ge(h2T_act, 1)
            pe.wait_ge(h2T_dve, 1)
            pe.wait_ge(wr_in, 32)
            pe.wait_ge(ones_set, 1)
            for t in range(NT):
                for k in range(KD):
                    last = mm(bank[4][:, t * HD:t * HD + LG], h2T[:, k, t * P:(t + 1) * P], wr[:, k, :],
                              start=(k == 0), stop=(k == KD - 1))
            last.then_inc(logits_done, 1)
            pe.wait_ge(member_ready, 1)
            mm(bank[5][:, 0:E], before, member[:, 0, :], start=True, stop=True)
            mm(bank[5][:, E:2 * E], onesb, member[:, 0, :], start=True, stop=False)
            mm(bank[5][:, E:2 * E], before, member[:, 1, :], start=False, stop=True)
            mm(bank[5][:, 2 * E:3 * E], onesb, member[:, 0, :], start=True, stop=False)
            mm(bank[5][:, 2 * E:3 * E], onesb, member[:, 1, :], start=False, stop=True).then_inc(rank_done, 1)

            def gather():
                for k in range(KD):
                    for t in range(NT):
                        for i in range(3):
                            mm(p_hg[:, k * CAP:(k + 1) * CAP], hs[:, i, t, k, :], selb[:, t, :],
                               start=(t == 0 and i == 0), stop=(t == NT - 1 and i == 2))

            def transpose_weights():
                for t in range(NT):
                    last = nc.tensor.transpose(p_tr[:, t * P:(t + 1) * P], selw[:, t, :], ident)
                last.then_inc(gathered, 1)

            def add_back(b, stop=False):
                for t in range(NT):
                    for half in range(2):
                        last = mm(acc[t][half][:, :], selT[b][HD * half:HD * (half + 1), t * P:(t + 1) * P],
                                  yb[b][HD * half:HD * (half + 1), :], start=False, stop=stop)
                return last

            pe.wait_ge(split_ready, 1)
            pe.wait_ge(sel_ready, 1)
            gather()
            transpose_weights()

            def expert(n, turn, s):
                pe.wait_ge(hg_ready, n + 1)
                pe.wait_ge(slot_in[s], turn * 48 + 48)
                for k in range(KD):
                    for h in range(2):
                        last = mm(p_gu[HD * h:HD * (h + 1), 0:FE], hg[:, k, :], s_gu[s][:, :, k, h, :],
                                  start=(k == 0), stop=(k == KD - 1))
                last.then_inc(gu_done, 1)
                pe.wait_ge(sel_ready, n + 2)
                gather()
                pe.wait_ge(selT_ready, n + 1)
                transpose_weights()
                pe.wait_ge(act_ready, n + 1)
                nc.tensor.transpose(p_tr[:, 2 * P:3 * P], act_sb, ident).then_inc(actt_done, 1)
                pe.wait_ge(y_ready, n + 1)
                add_back((s + 1) % 2).then_inc(added, 1)
                pe.wait_ge(actT_ready, n + 1)
                for f in range(2):
                    for half in range(2):
                        last = mm(p_y[HD * half:HD * (half + 1), :], actT[:, HD * f:HD * (f + 1)],
                                  s_dn[s][:, f, half * HALF:(half + 1) * HALF], start=(f == 0), stop=(f == 1))
                last.then_inc(down_done, 1)

            pe.wait_ge(rounds_ready, 1)
            rounds = pe.value_load(rounds_i[0:1, 0:1], min_val=1, max_val=ROUNDS_MAX)
            with pe.Fori(0, rounds) as r:
                with pe.Fori(0, LOOPS) as g:
                    for s in range(NSLOT):
                        expert(r * E + g * NSLOT + s, r * (LOOPS + (s < TAIL)) + g, s)
                for s in range(TAIL):
                    expert(r * E + (LOOPS * NSLOT + s), r * (LOOPS + 1) + LOOPS, s)
            pe.wait_ge(y_ready, rounds * E + 1)
            add_back(1, stop=True).then_inc(acc_done, 1)

        @block.scalar
        def _(act):
            A = nc.scalar.activation
            steps = [0]

            def step(ins):
                steps[0] += 1
                ins.then_inc(act_step, 1)
                act.wait_ge(act_step, steps[0])

            act.dma_start(cf[:, :], I["const_f32"]).then_inc(cst_in, 16)
            act.dma_start(cb[:, :], I["const_bf16"]).then_inc(cst_in, 16)
            act.dma_start(neg8, I["const_neg8"]).then_inc(cst_in, 16)
            act.dma_start(gvec[0:KD, :], I["norm_mix_g"][0].rearrange("(k p) -> k p", p=P)).then_inc(gv_in, 16)
            act.dma_start(gvec[KD:KD + 4, :], I["fox_out_g"][0].rearrange("(k p) -> k p", p=P)).then_inc(gv_in, 16)
            act.dma_start(gvec[KD + 4:2 * KD, :], I["moba_out_g"][0].rearrange("(k p) -> k p", p=P)).then_inc(gv_in, 16)
            act.dma_start(bfg, I["b_forget"][0].rearrange("(h o) -> h o", o=1)).then_inc(gv_in, 16)
            act.wait_ge(ones_set, 1)
            act.dma_start(wr[:, :, 0:N_GROUPS], I["w_router_group"][0].rearrange("(k p) g -> p k g", p=P)).then_inc(wr_in, 16)
            act.dma_start(wr[:, :, 8:LG], I["w_router_expert"][0].rearrange("(k p) g e -> p k (g e)", p=P)).then_inc(wr_in, 16)

            def squares(n, dst):
                for t in range(NT):
                    last = A(dst[:, t, :], x[:, t, :], ACT.Square, accum_out=ssq[:, t:t + 1])
                last.then_inc(ssq_ready, 1)

            def seed_rsqrt(k):
                act.wait_ge(var_ready, k + 1)
                step(A(seed, var, ACT.Ln))
                A(seed, seed, ACT.Exp, scale=-0.5).then_inc(seed_ready, 1)

            act.wait_ge(x_in, 16 * NT)
            squares(0, xn)
            seed_rsqrt(0)
            act.wait_ge(gcol_t, 1)
            nc.scalar.copy(gcol[:, :], bank[0][:, 0:2 * KD]).then_inc(gcol_set, 1)
            act.wait_ge(gcol_set, 1)
            for i in range(2):
                act.wait_ge(tr_done, i + 1)
                for k in (2 * i, 2 * i + 1):
                    last = A(hT[:, k, :], bank[4 + i][:, (k % 2) * SEQ:(k % 2 + 1) * SEQ], ACT.Copy, scale=gcol[:, k:k + 1])
            last.then_inc(hT_act, 1)

            def took(g, dst, src):
                act.wait_ge(grp_done, g + 1)
                nc.scalar.copy(dst, src).then_inc(act_took, 1)

            act.wait_ge(gv_in, 64)
            act.wait_ge(grp_done, 1)
            A(fz, grp_bank(G_FT)[0:N_FOX, 0:SEQ], ACT.Identity, bias=bfg).then_inc(act_took, 1)
            act.wait_ge(fa_ready, 1)
            step(A(fl, fa, ACT.Exp, scale=-1.0))
            A(fl, fl, ACT.Ln, bias=1.0).then_inc(fl_ready, 1)
            for i in range(4):
                g = G_FQK + i
                a = (PAIRS if i >= 2 else 0) + 2 * (i % 2)
                took(g, qk[:, a:a + 2, :].rearrange("p a b -> p (a b)"), grp_bank(g)[:, :])
            for t in range(NT):
                took(G_FV + t, v[:, t, 0:FOX_W], grp_bank(G_FV + t)[:, :])

            def exps(j):
                act.wait_ge(nm_ready, j + 1)
                for h in range(2):
                    for t in range(NT):
                        c, nk = t * P, (t + 1) * P
                        last = A(prob[j % 2][h][:, c:c + nk], bank[4 + 2 * (j % 2) + h][:, c:c + nk], ACT.Exp,
                                 bias=nm[j % 2][:, 2 * h + t:2 * h + t + 1], scale=SCALE,
                                 accum_out=rs[j % 2][:, 2 * h + t:2 * h + t + 1])
                last.then_inc(exp_done, 1)

            def take_probT(j):
                act.wait_ge(t_done, j + 1)
                nc.scalar.copy(probT[j % 2][0], bank[4 + 2 * (j % 2)][:, 0:PW]).then_inc(pt_act, 1)

            def take_o(j):
                act.wait_ge(o_done, j + 1)
                nc.scalar.copy(oT[:, j, :], bank[O_BANK][:, 0:SEQ]).then_inc(o_taken, 1)

            def take_mqk(g):
                w, t = (g - G_MQ) // 2, (g - G_MQ) % 2
                took(g, mqk[:, w, t, :], grp_bank(g)[:, :])

            exps(0)
            exps(1)
            take_mqk(G_MQ)
            take_probT(0)
            take_probT(1)
            take_mqk(G_MQ + 1)
            take_o(0)
            take_o(1)
            exps(2)
            exps(3)
            take_mqk(G_MK)
            take_probT(2)
            take_probT(3)
            take_mqk(G_MK + 1)
            take_o(2)
            take_o(3)
            took(G_MV, v[:, 0, FOX_W:], grp_bank(G_MV)[:, :])
            act.wait_ge(xt_done, 1)
            for i in range(2):
                last = nc.scalar.copy(qT[:, 4 + 2 * i:6 + 2 * i, :].rearrange("p a b -> p (a b)"), bank[4 + i][:, :])
            last.then_inc(xt_act, 1)
            took(G_MV + 1, v[:, 1, FOX_W:], grp_bank(G_MV + 1)[:, :])
            act.dma_start(gffn, I["norm_ffn_g"].to_broadcast([P, D])).then_inc(gains_in, 16)
            act.dma_start(gfin, I["norm_final_g"].rearrange("(o d) -> o d", o=1).to_broadcast([P, D])).then_inc(gains_in, 16)
            exps(4)
            exps(5)
            seed_rsqrt(1)
            take_probT(4)
            take_probT(5)
            take_o(4)
            take_o(5)
            exps(6)
            exps(7)
            take_probT(6)
            take_probT(7)
            take_o(6)
            take_o(7)
            seed_rsqrt(2)
            act.wait_ge(grp_done, G_OM + 4)
            act.dma_start(biasb[:, 0:N_GROUPS], I["b_router_group"].to_broadcast([P, N_GROUPS])).then_inc(gains_in, 16)
            act.dma_start(biasb[:, 8:LG], I["b_router_expert"].rearrange("o g e -> o (g e)").to_broadcast([P, E])).then_inc(gains_in, 16)
            act.wait_ge(x1_ready, 1)
            squares(3, res.rearrange("p t k c -> p t (k c)"))
            seed_rsqrt(3)
            def permuted(t):
                return h2[:, t, :].rearrange("p (c k) -> p k c", k=KD)

            act.wait_ge(h2_ready, NT)
            for t in range(NT):
                last = nc.scalar.copy(hs[:, 0, t, :, :], permuted(t))
            last.then_inc(hi_ready, 1)
            act.wait_ge(h2t_done, 2)
            for i in range(2):
                last = nc.scalar.copy(h2T[:, 2 * i:2 * i + 2, :].rearrange("p a b -> p (a b)"), bank[4 + i][:, :])
            last.then_inc(h2T_act, 1)
            act.wait_ge(r1_ready, 1)
            for t in range(NT):
                last = nc.scalar.copy(hs[:, 1, t, :, :], res[:, t, :, :])
            last.then_inc(mid_ready, 1)
            act.wait_ge(gm_ready, 1)
            for t in range(NT):
                last = A(gexp[:, t, :], lg[:, t, 0:8], ACT.Exp, bias=one[t][0], accum_out=one[t][1])
            last.then_inc(gexp_done, 1)
            act.wait_ge(ed_ready, 1)
            for t in range(NT):
                last = A(one[t][3], etop8[:, t, 1:2], ACT.Exp, bias=one[t][2])
            last.then_inc(eexp_done, 1)

            def take_selT(n, b):
                act.wait_ge(gathered, n + 1)
                nc.scalar.copy(selT[b], p_tr[:, 0:SEQ]).then_inc(selT_ready, 1)

            take_selT(0, 0)

            def expert(n, s):
                act.wait_ge(gu_done, n + 1)
                A(sig, p_gu[:, 0:P], ACT.Sigmoid).then_inc(sig_ready, 1)
                act.wait_ge(actt_done, n + 1)
                nc.scalar.copy(actT, p_tr[:, 2 * P:3 * P]).then_inc(actT_ready, 1)
                act.wait_ge(added, n + 1)
                take_selT(n + 1, (s + 1) % 2)
                act.wait_ge(down_done, n + 1)
                nc.scalar.copy(yb[s % 2], p_y[:, :]).then_inc(y_ready, 1)

            act.wait_ge(rounds_ready, 1)
            rounds = act.value_load(rounds_i[0:1, 0:1], min_val=1, max_val=ROUNDS_MAX)
            with act.Fori(0, rounds) as r:
                with act.Fori(0, LOOPS) as g:
                    for s in range(NSLOT):
                        expert(r * E + g * NSLOT + s, s)
                for s in range(TAIL):
                    expert(r * E + (LOOPS * NSLOT + s), s)
            act.wait_ge(acc_done, 1)
            for t in range(NT):
                for half in range(2):
                    last = A(outb[t][:, half * HALF:(half + 1) * HALF], acc[t][half][:, :], ACT.Square,
                             accum_out=one[t][4 + half])
            last.then_inc(ssq_ready, 1)
            seed_rsqrt(4)

        @block.gpsimd
        def _(pool):
            steps = [0]

            def step(ins):
                steps[0] += 1
                ins.then_inc(pool_step, 1)
                pool.wait_ge(pool_step, steps[0])

            def rotate(g):
                w, t = (g - G_MQ) // 2, (g - G_MQ) % 2
                pool.wait_ge(act_took, g + 1)
                heads = mqk[:, w, t, :].rearrange("p (h c) -> p h c", h=N_MOBA)
                t1, t2 = heads[:, :, 0:ROT], heads[:, :, ROT:2 * ROT]
                cos = cf[:, C_COS + t * ROT:C_COS + (t + 1) * ROT].unsqueeze(1).to_broadcast([P, N_MOBA, ROT])
                sin = cf[:, C_SIN + t * ROT:C_SIN + (t + 1) * ROT].unsqueeze(1).to_broadcast([P, N_MOBA, ROT])
                for i, (a, b) in enumerate(((t1, cos), (t2, sin), (t2, cos), (t1, sin))):
                    last = nc.gpsimd.tensor_tensor(ropet[:, i], a, b, ALU.mult)
                step(last)
                nc.gpsimd.tensor_tensor(t1, ropet[:, 0], ropet[:, 1], ALU.subtract)
                last = nc.gpsimd.tensor_tensor(t2, ropet[:, 2], ropet[:, 3], ALU.add)
                step(last)
                pool.sem_inc(rope_done, 1)

            def square_and_scale(j):
                group = j // FOX_PAIRS
                pool.wait_ge(o_taken, j + 1)
                if j % FOX_PAIRS == 0:
                    step(nc.gpsimd.tensor_tensor(sqacc[:, group, :], oT[:, j, :], oT[:, j, :], ALU.mult))
                else:
                    step(nc.gpsimd.tensor_tensor(sqt, oT[:, j, :], oT[:, j, :], ALU.mult))
                    step(nc.gpsimd.tensor_tensor(sqacc[:, group, :], sqacc[:, group, :], sqt, ALU.add))
                nc.gpsimd.tensor_scalar(oT[:, j, :], oT[:, j, :], gcol[:, KD + j:KD + j + 1], None, ALU.mult).then_inc(o_ready, 1)

            pool.wait_ge(cst_in, 48)
            pool.wait_ge(gcol_set, 1)
            rotate(G_MQ)
            rotate(G_MQ + 1)
            square_and_scale(0)
            square_and_scale(1)
            rotate(G_MK)
            rotate(G_MK + 1)
            for j in range(2, PAIRS):
                square_and_scale(j)
            pool.wait_ge(hi_ready, 1)
            for t in range(NT):
                last = nc.gpsimd.tensor_tensor(res[:, t, :, :], h2[:, t, :].rearrange("p (c k) -> p k c", k=KD),
                                               hs[:, 0, t, :, :], ALU.subtract)
            last.then_inc(r1_ready, 1)
            pool.wait_ge(mid_ready, 1)
            pool.wait_ge(r1_ready, 1)
            for t in range(NT):
                last = nc.gpsimd.tensor_tensor(hs[:, 2, t, :, :], res[:, t, :, :], hs[:, 1, t, :, :], ALU.subtract)
            last.then_inc(split_ready, 1)
            pool.wait_ge(logits_done, 1)
            nc.gpsimd.memset(yb[1], 0.0)
            nc.gpsimd.memset(selT[1], 0.0).then_inc(y_ready, 1)

        @block.vector
        def _(dve):
            V = nc.vector
            steps = [0]

            def step(ins):
                steps[0] += 1
                ins.then_inc(dve_step, 1)
                dve.wait_ge(dve_step, steps[0])

            V.memset(onescol, 1.0)
            V.memset(wr[:, :, N_GROUPS:8], 0.0).then_inc(ones_set, 1)

            def variance(k, total, width):
                step(V.tensor_scalar(var, total, 1.0 / width, EPS, ALU.mult, ALU.add))
                dve.sem_inc(var_ready, 1)

            def refine_rsqrt(k):
                dve.wait_ge(seed_ready, k + 1)
                step(V.scalar_tensor_tensor(out=rt, in0=seed, scalar=-0.5, in1=seed, op0=ALU.mult, op1=ALU.mult))
                step(V.tensor_tensor(rt, rt, var, ALU.mult))
                step(V.scalar_tensor_tensor(out=rstd, in0=rt, scalar=1.5, in1=seed, op0=ALU.add, op1=ALU.mult))

            dve.wait_ge(ssq_ready, 1)
            variance(0, ssq, D)
            refine_rsqrt(0)
            for t in range(NT):
                V.tensor_scalar(xn[:, t, :], x[:, t, :], rstd[:, t:t + 1], None, ALU.mult).then_inc(xn_ready, 1)
            dve.wait_ge(gcol_set, 1)
            for i in range(2, 4):
                dve.wait_ge(tr_done, i + 1)
                for k in (2 * i, 2 * i + 1):
                    last = V.tensor_scalar(hT[:, k, :], bank[4 + i][:, (k % 2) * SEQ:(k % 2 + 1) * SEQ], gcol[:, k:k + 1], None, ALU.mult)
            last.then_inc(hT_dve, 1)
            dve.wait_ge(act_took, 1)
            V.scalar_tensor_tensor(out=fa, in0=fz, scalar=-1.0, in1=fz, op0=ALU.mult, op1=ALU.max).then_inc(fa_ready, 1)
            dve.wait_ge(fl_ready, 1)
            step(V.scalar_tensor_tensor(out=fz, in0=fz, scalar=0.0, in1=fl, op0=ALU.min, op1=ALU.subtract))
            V.tensor_tensor_scan(fc, fz, fz, 0.0, ALU.add, ALU.bypass).then_inc(fc_ready, 1)

            def maxima(j):
                dve.wait_ge(s_done, j + 1)
                for h in range(2):
                    for t in range(NT):
                        c, nk = t * P, (t + 1) * P
                        last = V.reduce_max(mx[j % 2][:, 2 * h + t:2 * h + t + 1], bank[4 + 2 * (j % 2) + h][:, c:c + nk], AX)
                step(last)
                V.tensor_scalar(nm[j % 2], mx[j % 2], -SCALE, None, ALU.mult).then_inc(nm_ready, 1)

            def normalise(j):
                dve.wait_ge(exp_done, j + 1)
                step(V.reciprocal(rs[j % 2], rs[j % 2]))
                for h in range(2):
                    for t in range(NT):
                        c, nk = t * P, (t + 1) * P
                        p = prob[j % 2][h][:, c:c + nk]
                        last = V.tensor_scalar(p, p, rs[j % 2][:, 2 * h + t:2 * h + t + 1], None, ALU.mult)
                last.then_inc(p_ready, 1)

            def take_probT(j):
                dve.wait_ge(t_done, j + 1)
                V.tensor_copy(probT[j % 2][1], bank[5 + 2 * (j % 2)][:, 0:PW]).then_inc(pt_dve, 1)

            def add_projection(g, t, half):
                dve.wait_ge(grp_done, g + 1)
                xs = x[:, t, half * HALF:(half + 1) * HALF]
                V.scalar_tensor_tensor(out=xs, in0=grp_bank(g)[:, :], scalar=rstd[:, t:t + 1], in1=xs,
                                       op0=ALU.mult, op1=ALU.add).then_inc(dve_took, 1)

            def group_variance(k, g):
                dve.wait_ge(grp_done, g + 1)
                step(V.tensor_scalar(var, grp_bank(g)[:, 0:NT], 1.0 / FOX_W, EPS, ALU.mult, ALU.add))
                dve.sem_inc(var_ready, 1)
                dve.sem_inc(dve_took, 1)

            maxima(0)
            maxima(1)
            normalise(0)
            normalise(1)
            take_probT(0)
            take_probT(1)
            maxima(2)
            maxima(3)
            normalise(2)
            normalise(3)
            take_probT(2)
            take_probT(3)
            dve.wait_ge(xt_done, 1)
            for i in range(2):
                last = V.tensor_copy(kT[:, 4 + 2 * i:6 + 2 * i, :].rearrange("p a b -> p (a b)"), bank[6 + i][:, :])
            last.then_inc(xt_dve, 1)
            maxima(4)
            maxima(5)
            group_variance(1, G_SF)
            normalise(4)
            normalise(5)
            refine_rsqrt(1)
            add_projection(G_OF, 0, 0)
            add_projection(G_OF + 1, 0, 1)
            take_probT(4)
            take_probT(5)
            add_projection(G_OF + 2, 1, 0)
            maxima(6)
            maxima(7)
            normalise(6)
            normalise(7)
            add_projection(G_OF + 3, 1, 1)
            take_probT(6)
            take_probT(7)
            group_variance(2, G_SM)
            refine_rsqrt(2)
            dve.wait_ge(dve_took, 5)
            for i in range(4):
                add_projection(G_OM + i, i // 2, i % 2)
            dve.wait_ge(dve_took, 10)
            dve.sem_inc(x1_ready, 1)
            dve.wait_ge(ssq_ready, 2)
            variance(3, ssq, D)
            refine_rsqrt(3)
            dve.wait_ge(gains_in, 64)
            V.memset(biasb[:, N_GROUPS:8], NEG)
            for t in range(NT):
                V.scalar_tensor_tensor(out=h2[:, t, :], in0=x[:, t, :], scalar=rstd[:, t:t + 1], in1=gffn,
                                       op0=ALU.mult, op1=ALU.mult).then_inc(h2_ready, 1)
            dve.wait_ge(h2t_done, 4)
            for i in range(2, 4):
                last = V.tensor_copy(h2T[:, 2 * i:2 * i + 2, :].rearrange("p a b -> p (a b)"), bank[4 + i][:, :])
            last.then_inc(h2T_dve, 1)

            dve.wait_ge(logits_done, 1)
            for t in range(NT):
                last = V.tensor_tensor(lg[:, t, :], bank[4][:, t * HD:t * HD + LG], biasb, ALU.add)
            step(last)
            for t in range(NT):
                last = V.max(top8[:, t, :], lg[:, t, 0:8])
            step(last)
            for t in range(NT):
                last = V.tensor_scalar(one[t][0], top8[:, t, 0:1], -1.0, None, ALU.mult)
            last.then_inc(gm_ready, 1)
            for t in range(NT):
                last = V.max_index(idx8[:, t, :], top8[:, t, :], lg[:, t, 0:8])
            step(last)
            for t in range(NT):
                last = V.tensor_copy(one[t][6], idx8[:, t, 0:1])
            step(last)
            for t in range(NT):
                last = V.tensor_scalar(gmask[:, t, :], iota[:, 0:N_GROUPS], one[t][6], None, ALU.is_equal)
            step(last)
            for g in range(N_GROUPS):
                for t in range(NT):
                    e8 = lg[:, t, 8 + EPG * g:8 + EPG * (g + 1)]
                    if g == 0:
                        last = V.tensor_scalar(el8[:, t, :], e8, gmask[:, t, 0:1], None, ALU.mult)
                    else:
                        last = V.scalar_tensor_tensor(out=el8[:, t, :], in0=e8, scalar=gmask[:, t, g:g + 1], in1=el8[:, t, :],
                                                      op0=ALU.mult, op1=ALU.add)
                step(last)
            for t in range(NT):
                last = V.max(etop8[:, t, :], el8[:, t, :])
            step(last)
            for t in range(NT):
                last = V.tensor_scalar(one[t][2], etop8[:, t, 0:1], -1.0, None, ALU.mult)
            last.then_inc(ed_ready, 1)
            for t in range(NT):
                last = V.max_index(eidx8[:, t, :], etop8[:, t, :], el8[:, t, :])
            step(last)
            for t in range(NT):
                V.tensor_copy(one[t][4], eidx8[:, t, 0:1])
                last = V.tensor_copy(one[t][5], eidx8[:, t, 1:2])
            step(last)
            for t in range(NT):
                for i in (4, 5):
                    last = V.scalar_tensor_tensor(out=one[t][i], in0=one[t][6], scalar=float(EPG), in1=one[t][i],
                                                  op0=ALU.mult, op1=ALU.add)
            step(last)
            for t in range(NT):
                last = V.tensor_scalar(memf[:, t, :], iota[:, 0:E], one[t][4], None, ALU.is_equal)
            step(last)
            for t in range(NT):
                last = V.scalar_tensor_tensor(out=memf[:, t, :], in0=iota[:, 0:E], scalar=one[t][5], in1=memf[:, t, :],
                                              op0=ALU.is_equal, op1=ALU.add)
            step(last)
            step(V.tensor_copy(member[:, :, :], memf[:, :, :]))
            dve.sem_inc(member_ready, 1)
            dve.wait_ge(gexp_done, 1)
            dve.wait_ge(eexp_done, 1)
            for t in range(NT):
                last = V.tensor_scalar(one[t][7], one[t][3], 1.0, one[t][1], ALU.add, ALU.mult)
            step(last)
            for t in range(NT):
                last = V.reciprocal(one[t][7], one[t][7])
            step(last)
            for t in range(NT):
                last = V.tensor_tensor(one[t][8], one[t][7], one[t][3], ALU.mult)
            step(last)
            for t in range(NT):
                V.tensor_scalar(wgt[:, t, :], iota[:, 0:E], one[t][4], one[t][7], ALU.is_equal, ALU.mult)
                last = V.tensor_scalar((wa, wb)[t], iota[:, 0:E], one[t][5], one[t][8], ALU.is_equal, ALU.mult)
            step(last)
            for t in range(NT):
                last = V.tensor_tensor(wgt[:, t, :], wgt[:, t, :], (wa, wb)[t], ALU.add)
            step(last)
            dve.wait_ge(rank_done, 1)
            for t in range(NT):
                last = V.scalar_tensor_tensor(out=rank[:, t, :], in0=bank[5][:, t * E:(t + 1) * E], scalar=1.0, in1=memf[:, t, :],
                                              op0=ALU.add, op1=ALU.mult)
            step(last)
            step(V.tensor_scalar(rank[:, :, :], rank[:, :, :], -1.0, None, ALU.add))
            step(V.reduce_max(most, bank[5][:, 2 * E:3 * E], AX))
            step(V.tensor_scalar(nrounds, most, float(CAP), 1.0, ALU.is_gt, ALU.add))
            for m in range(2, ROUNDS_MAX):
                step(V.scalar_tensor_tensor(out=nrounds, in0=most, scalar=float(CAP * m), in1=nrounds, op0=ALU.is_gt, op1=ALU.add))
            step(V.tensor_copy(rounds_i, nrounds))
            dve.sem_inc(rounds_ready, 1)

            def select(e):
                for t in range(NT):
                    at = rank[:, t, e:e + 1] if isinstance(e, int) else rank[:, t, bass.ds(e, 1)]
                    w = wgt[:, t, e:e + 1] if isinstance(e, int) else wgt[:, t, bass.ds(e, 1)]
                    V.tensor_scalar(selb[:, t, :], iota[:, 0:CAP], at, None, ALU.is_equal)
                    last = V.tensor_scalar(selw[:, t, :], iota, at, w, ALU.is_equal, ALU.mult)
                last.then_inc(sel_ready, 1)

            def take_gathered(n):
                dve.wait_ge(gathered, n + 1)
                V.tensor_copy(hg[:, :, :].rearrange("p k c -> p (k c)"), p_hg[:, :]).then_inc(hg_ready, 1)

            select(0)
            take_gathered(0)
            moe_step0 = steps[0]
            PER_EXPERT, PER_ROUND = 1, E + 1

            def expert(n, e_next, s, own):
                if isinstance(e_next, int) and e_next == E:
                    V.tensor_scalar(rank[:, :, :], rank[:, :, :], -float(CAP), None, ALU.add).then_inc(dve_step, 1)
                    dve.wait_ge(dve_step, own + (moe_step0 + 1))
                    own, e_next = own + 1, 0
                select(e_next)
                dve.wait_ge(sig_ready, n + 1)
                V.tensor_tensor(gated, p_gu[:, 0:P], sig, ALU.mult).then_inc(dve_step, 1)
                dve.wait_ge(dve_step, own + (moe_step0 + 1))
                V.tensor_tensor(act_sb, p_gu[:, P:2 * P], gated, ALU.mult).then_inc(act_ready, 1)
                take_gathered(n + 1)

            rounds = dve.value_load(rounds_i[0:1, 0:1], min_val=1, max_val=ROUNDS_MAX)
            with dve.Fori(0, rounds) as r:
                with dve.Fori(0, LOOPS) as g:
                    for s in range(NSLOT):
                        expert(r * E + g * NSLOT + s, g * NSLOT + (s + 1), s, r * PER_ROUND + g * NSLOT + s)
                for s in range(TAIL):
                    e = LOOPS * NSLOT + s
                    expert(r * E + e, e + 1, s, r * PER_ROUND + e)

            steps[0] = 0
            own = rounds * PER_ROUND + moe_step0
            dve.wait_ge(ssq_ready, 3)
            for t in range(NT):
                last = V.tensor_tensor(ssq[:, t:t + 1], one[t][4], one[t][5], ALU.add)
            last.then_inc(dve_step, 1)
            dve.wait_ge(dve_step, own + 1)
            V.tensor_scalar(var, ssq, 1.0 / D, EPS, ALU.mult, ALU.add).then_inc(var_ready, 1)
            dve.wait_ge(seed_ready, 5)
            V.scalar_tensor_tensor(out=rt, in0=seed, scalar=-0.5, in1=seed, op0=ALU.mult, op1=ALU.mult).then_inc(dve_step, 1)
            dve.wait_ge(dve_step, own + 2)
            V.tensor_tensor(rt, rt, var, ALU.mult).then_inc(dve_step, 1)
            dve.wait_ge(dve_step, own + 3)
            V.scalar_tensor_tensor(out=rstd, in0=rt, scalar=1.5, in1=seed, op0=ALU.add, op1=ALU.mult).then_inc(dve_step, 1)
            dve.wait_ge(dve_step, own + 4)
            for t in range(NT):
                for half in range(2):
                    c = slice(half * HALF, (half + 1) * HALF)
                    last = V.scalar_tensor_tensor(out=outb[t][:, c], in0=acc[t][half][:, :], scalar=rstd[:, t:t + 1], in1=gfin[:, c],
                                                  op0=ALU.mult, op1=ALU.mult)
                last.then_inc(fin_ready, 1)


_INS = ["x", "norm_mix_g", "w_in", "b_forget", "fox_out_g", "moba_out_g", "w_out", "norm_ffn_g", "w_router_group",
        "b_router_group", "w_router_expert", "b_router_expert", "w_gate", "w_up", "w_down", "norm_final_g"]


def constants(np, bf16):
    half = ROT
    inv = (np.float32(500000.0) ** (-np.arange(half, dtype=np.float32) / np.float32(half))).astype(np.float32)
    ang = np.arange(SEQ, dtype=np.float32)[:, None] * inv[None, :]
    f = np.zeros((P, C_END), np.float32)
    f[:, C_ID:C_ID + P] = np.eye(P)
    f[:, C_IOTA:C_IOTA + P] = np.arange(P) % CAP
    for t in range(NT):
        f[:, C_COS + t * ROT:C_COS + (t + 1) * ROT] = np.cos(ang[t * P:(t + 1) * P])
        f[:, C_SIN + t * ROT:C_SIN + (t + 1) * ROT] = np.sin(ang[t * P:(t + 1) * P])
    b = np.zeros((P, 4 * P), np.float32)
    b[:, 0:P] = np.eye(P)
    b[:, P:2 * P] = np.triu(np.full((P, P), -1e30), 1)
    b[:, 2 * P:3 * P] = np.triu(np.ones((P, P)), 1)
    b[:, 3 * P:4 * P] = 1.0
    n8 = np.zeros((N_FOX, N_FOX, P), np.float32)
    for h in range(N_FOX):
        n8[h, h, :] = -1.0 / SCALE
    return {"const_f32": f, "const_bf16": b.astype(bf16), "const_neg8": n8}


def kernel(**inputs):
    import numpy as np
    import concourse.bacc as bacc
    from concourse.bass_utils import run_bass_kernel_spmd

    nc = bacc.Bacc("TRN2", target_bir_lowering=False, num_devices=1)
    arrays, args = {}, {}
    given = {n: np.ascontiguousarray(inputs[n]) for n in _INS}
    given.update(constants(np, mybir.dt.np(mybir.dt.bfloat16)))
    for name, a in given.items():
        arrays[f"in_{name}_dram"] = a
        args[name] = nc.dram_tensor(f"in_{name}_dram", a.shape, mybir.dt.from_np(a.dtype), kind="ExternalInput").ap()
    out = nc.dram_tensor("out_0_dram", (1, SEQ, D), mybir.dt.float32, kind="ExternalOutput").ap()
    layer_program(nc, args, out)
    r = run_bass_kernel_spmd(nc, [arrays], core_ids=[0])
    return r.results[0]["out_0_dram"]
```

```python
import concourse.bass as bass
from concourse import mybir
from contextlib import ExitStack

P = 128
SEQ = 256
D = 1024
HD = 64
NT = SEQ // P
KD = D // P
FOX_W = 512
MOBA_W = 512
N_FOX = FOX_W // HD
N_MOBA = MOBA_W // HD
MIX_W = FOX_W + MOBA_W
PAIRS = MIX_W // P
FOX_PAIRS = FOX_W // P
ROT = HD // 8
N_GROUPS = 4
EPG = 8
E = N_GROUPS * EPG
FE = 256
EPS = 1e-6
SCALE = HD ** -0.5
HALF = 512
CAP = 32
CP = 2 * CAP
COUPLES = E // 2
PASSES_MAX = SEQ // CAP
NSLOT = 3
EXPERT = 3 * KD * FE
SLOT = 2 * EXPERT
LOOPS = COUPLES // NSLOT
TAIL = COUPLES - LOOPS * NSLOT
ITEMS_MAX = COUPLES * PASSES_MAX
LG = 8 + E
LGP = 64
NEG = -3.0e38
C_ID, C_IOTA, C_COS, C_SIN, C_END = 0, P, 2 * P, 2 * P + NT * ROT, 2 * P + 2 * NT * ROT


def layer_program(nc, I, out):
    fp32, bf16 = mybir.dt.float32, mybir.dt.bfloat16
    i32, u32 = mybir.dt.int32, mybir.dt.uint32
    ALU, ACT, AX = mybir.AluOpType, mybir.ActivationFunctionType, mybir.AxisListType.X
    ctx = ExitStack()
    with ctx:
        def sb(name, shape, dt=fp32):
            return ctx.enter_context(nc.sbuf_tensor(name, shape, dt))

        def sem(name):
            return ctx.enter_context(nc.semaphore(name))

        ring = sb("ring", [P, NSLOT * SLOT])
        x = sb("x", [P, NT, D])
        hT = sb("hT", [P, KD, SEQ])
        qk = sb("qk", [P, 2 * PAIRS, SEQ])
        v = sb("v", [P, NT, MIX_W])
        stage = sb("stage", [P, NT * D])
        pp = sb("pp", [P, 3072])
        cf = sb("cf", [P, C_END])
        cb = sb("cb", [P, 4 * P], bf16)
        gcol = sb("gcol", [P, 2 * KD])
        add2 = sb("add2", [P, LG])
        stats = sb("stats", [P, 40])

        ident, iota = cf[:, C_ID:C_ID + P], cf[:, C_IOTA:C_IOTA + P]
        identb, causal = cb[:, 0:P], cb[:, P:2 * P]
        before, onesb = cb[:, 2 * P:3 * P], cb[:, 3 * P:4 * P]
        qT, kT = qk[:, 0:PAIRS, :], qk[:, PAIRS:2 * PAIRS, :]
        oT = qT
        xn = stage[:, :].rearrange("p (t d) -> p t d", t=NT)
        mqk = stage[:, :].rearrange("p (w t c) -> p w t c", w=2, t=NT)
        WI = KD * FOX_W
        w_blk = [ring[:, b * WI:(b + 1) * WI].rearrange("p (k c) -> p k c", k=KD) for b in range(6)]
        WO = 6 * WI
        w_o = ring[:, WO:WO + KD * D].rearrange("p (k c) -> p k c", k=KD)
        T0 = WO + KD * D
        wf = ring[:, T0:T0 + KD * N_FOX].rearrange("p (k c) -> p k c", k=KD)
        gvec = ring[0:2 * KD, T0 + 64:T0 + 64 + P]
        neg8 = ring[0:96, T0 + 192:T0 + 192 + N_FOX * P // 2].bitcast(bf16).rearrange("p (h c) -> p h c", h=N_FOX)
        cpart = ring[0:96, T0 + 704:T0 + 704 + SEQ // 2].bitcast(bf16)
        cmid = ring[0:N_FOX, T0 + 832:T0 + 832 + SEQ // 2].bitcast(bf16)
        ropet = ring[:, T0 + 1216:T0 + 1216 + 4 * N_MOBA * ROT].rearrange("p (i h r) -> p i h r", i=4, h=N_MOBA)
        sqt = ring[:, T0 + 1472:T0 + 1472 + SEQ]
        sqacc = ring[:, T0 + 1728:T0 + 1728 + 2 * SEQ].rearrange("p (g t) -> p g t", g=2)
        bfg = ring[0:N_FOX, T0 + 2240:T0 + 2241]
        fz, fa = v[0:N_FOX, 0, FOX_W:FOX_W + SEQ], v[0:N_FOX, 0, FOX_W + SEQ:MIX_W]
        fc, fl = v[0:N_FOX, 1, FOX_W:FOX_W + SEQ], v[0:N_FOX, 1, FOX_W + SEQ:MIX_W]
        PW = P + SEQ
        prob = [[pp[:, (2 * s + h) * PW:(2 * s + h + 1) * PW] for h in range(2)] for s in range(2)]
        probT = [[pp[:, (4 + 2 * s + h) * PW:(5 + 2 * s + h) * PW] for h in range(2)] for s in range(2)]
        ssq, var, seed, rstd, rt = (stats[:, 2 * i:2 * i + 2] for i in range(5))
        mx = [stats[:, 10 + 4 * s:14 + 4 * s] for s in range(2)]
        nm = [stats[:, 18 + 4 * s:22 + 4 * s] for s in range(2)]
        rs = [stats[:, 26 + 4 * s:30 + 4 * s] for s in range(2)]
        onescol = stats[:, 34:35]
        sq4 = stats[:, 35:39]
        warm = stats[:, 39:40]
        h2 = v
        h2T = hT
        res = pp[:, 0:NT * D].rearrange("p (t k c) -> p t k c", t=NT, k=KD)
        qkf = qk[:, :, :].rearrange("p a b -> p (a b)")
        hs = qkf[:, 0:3 * D].bitcast(bf16).rearrange("p (i t k c) -> p i t k c", i=3, t=NT, k=KD)
        gffn = stage[:, 0:D]
        wr = stage[:, D:D + KD * LGP].rearrange("p (k c) -> p k c", k=KD)
        lgT = stage[:, D + KD * LGP:D + KD * LGP + SEQ]
        gfin = v[:, 0, :]
        rtr = qkf[:, 3 * D:4 * D]
        cur = [0]

        def take(n, dt=fp32):
            cur[0] += n
            got = rtr[:, cur[0] - n:cur[0]]
            return got if dt is fp32 else got.bitcast(dt)

        lg = take(NT * LG).rearrange("p (t c) -> p t c", t=NT)
        biasb = take(LG)
        rank = take(NT * (E + 2)).rearrange("p (t e) -> p t e", t=NT)
        wgt = take(NT * E).rearrange("p (t e) -> p t e", t=NT)
        member = take(NT * E // 2, bf16).rearrange("p (t e) -> p t e", t=NT)
        memf = take(NT * E).rearrange("p (t e) -> p t e", t=NT)
        wa, wb = take(E), take(E)
        top8 = take(NT * 8).rearrange("p (t c) -> p t c", t=NT)
        idx8 = take(NT * 8, u32).rearrange("p (t c) -> p t c", t=NT)
        etop8 = take(NT * 8).rearrange("p (t c) -> p t c", t=NT)
        eidx8 = take(NT * 8, u32).rearrange("p (t c) -> p t c", t=NT)
        el8 = take(NT * 8).rearrange("p (t c) -> p t c", t=NT)
        gexp = take(NT * 8).rearrange("p (t c) -> p t c", t=NT)
        gmask = take(NT * N_GROUPS).rearrange("p (t c) -> p t c", t=NT)
        one = [[take(1) for _ in range(10)] for _ in range(NT)]
        most, passes = take(COUPLES), take(COUPLES, i32)
        base = take(COUPLES + 1, i32)
        hTf = hT[:, :, :].rearrange("p a b -> p (a b)")
        hg = hTf[:, 0:HALF].rearrange("p (k c) -> p k c", k=KD)
        yb = hTf[:, HALF:2 * HALF]
        selT = hTf[:, 2 * HALF:2 * HALF + SEQ]
        M0 = NT * D
        selw = pp[:, M0:M0 + NT * P].rearrange("p (t c) -> p t c", t=NT)
        selb = pp[:, M0 + 256:M0 + 320].bitcast(bf16).rearrange("p (t c) -> p t c", t=NT)
        act_sb = pp[:, M0 + 320:M0 + 448]
        sig, gated = pp[:, M0 + 448:M0 + 576], pp[:, M0 + 576:M0 + 704]
        actT = pp[:, M0 + 704:M0 + 832]
        slot = [ring[:, s * EXPERT:(s + 1) * EXPERT] for s in range(2 * NSLOT)]
        s_gu = [s[:, 0:2 * KD * FE].rearrange("p (w k h f) -> p w k h f", w=2, k=KD, h=2) for s in slot]
        s_dn = [s[:, 2 * KD * FE:].rearrange("p (h n) -> p h n", h=2) for s in slot]
        outb = [x[:, t, :] for t in range(NT)]

        bank = [ctx.enter_context(nc.psum_tensor(f"bank{i}", [P, HALF], fp32)) for i in range(8)]
        O_BANK = 3
        acc = [[bank[0], bank[1]], [bank[2], bank[3]]]
        p_hg, p_gu, p_tr, p_y = bank[4], bank[5], bank[6], bank[7]

        x_in, cst_in, wf_in, wo_in, gv_in, wr_in = (sem(n) for n in ("x_in", "cst_in", "wf_in", "wo_in", "gv_in", "wr_in"))
        fg_in, gffn_in, bias_in, gfin_in, add_in = (sem(n) for n in ("fg_in", "gffn_in", "bias_in", "gfin_in", "add_in"))
        blk_in = [sem(f"blk_in{b}") for b in range(6)]
        slot_in = [sem(f"slot_in{s}") for s in range(NSLOT)]
        out_done = sem("out_done")
        pool_step, dve_step, act_step = sem("pool_step"), sem("dve_step"), sem("act_step")
        ones_set, gcol_t, gcol_set = sem("ones_set"), sem("gcol_t"), sem("gcol_set")
        ssq_ready, var_ready, seed_ready, xn_ready = (sem(n) for n in ("ssq_ready", "var_ready", "seed_ready", "xn_ready"))
        tr_done, hT_act, hT_dve = sem("tr_done"), sem("hT_act"), sem("hT_dve")
        grp_done, act_took, dve_took = sem("grp_done"), sem("act_took"), sem("dve_took")
        fz_ready, fa_ready, fl_ready, fc_ready = (sem(n) for n in ("fz_ready", "fa_ready", "fl_ready", "fc_ready"))
        s_done, nm_ready, exp_done, p_ready, t_done = (sem(n) for n in ("s_done", "nm_ready", "exp_done", "p_ready", "t_done"))
        pt_act, pt_dve, o_done, o_taken, o_ready = (sem(n) for n in ("pt_act", "pt_dve", "o_done", "o_taken", "o_ready"))
        rope_done, xt_done, xt_act, xt_dve = (sem(n) for n in ("rope_done", "xt_done", "xt_act", "xt_dve"))
        h2_ready, h2t_done, lgT_done, lgT_ready = (sem(n) for n in ("h2_ready", "h2t_done", "lgT_done", "lgT_ready"))
        h2T_act, h2T_dve, logits_done = sem("h2T_act"), sem("h2T_dve"), sem("logits_done")
        gm_ready, gexp_done, ed_ready, eexp_done = (sem(n) for n in ("gm_ready", "gexp_done", "ed_ready", "eexp_done"))
        member_ready, rank_done, base_ready = sem("member_ready"), sem("rank_done"), sem("base_ready")
        hi_ready, r1_ready, mid_ready, split_ready = (sem(n) for n in ("hi_ready", "r1_ready", "mid_ready", "split_ready"))
        hg_ready, gu_done, sig_ready, sel_ready, selw_ready = (
            sem(n) for n in ("hg_ready", "gu_done", "sig_ready", "sel_ready", "selw_ready"))
        gathered, selT_ready, act_ready, actt_done = (sem(n) for n in ("gathered", "selT_ready", "act_ready", "actt_done"))
        actT_ready, down_done, y_ready, added = (sem(n) for n in ("actT_ready", "down_done", "y_ready", "added"))
        acc_done, fin_ready = sem("acc_done"), sem("fin_ready")

        G_FT, G_FQK, G_FV, G_MQ, G_MK, G_MV = 0, 1, 5, 7, 9, 11
        G_SF, G_OF, G_SM, G_OM = 13, 14, 18, 19

        def grp_bank(g):
            return bank[g % 3]

        def wait_bank_free(pe, g):
            if g >= 3:
                if g - 3 < G_SF:
                    pe.wait_ge(act_took, g - 2)
                else:
                    pe.wait_ge(dve_took, g - 3 - G_SF + 1)

        def pair_heads(j):
            return (2 * j, 2 * j + 1)

        block = ctx.enter_context(nc.Block())

        @block.sync
        def _(sp):
            for t in range(NT):
                sp.dma_start(x[:, t, :], I["x"][0, t * P:(t + 1) * P, :]).then_inc(x_in, 16)
            sp.dma_start(gvec[0:KD, :], I["norm_mix_g"][0].rearrange("(k p) -> k p", p=P)).then_inc(gv_in, 16)
            sp.dma_start(gvec[KD:KD + 4, :], I["fox_out_g"][0].rearrange("(k p) -> k p", p=P)).then_inc(gv_in, 16)
            sp.dma_start(gvec[KD + 4:2 * KD, :], I["moba_out_g"][0].rearrange("(k p) -> k p", p=P)).then_inc(gv_in, 16)
            sp.dma_start(wf, I["w_in"][0, :, 3 * FOX_W:3 * FOX_W + N_FOX].rearrange("(k p) c -> p k c", p=P)).then_inc(wf_in, 16)
            for b in range(6):
                c0 = b * FOX_W + (N_FOX if b >= 3 else 0)
                sp.dma_start(w_blk[b], I["w_in"][0, :, c0:c0 + FOX_W].rearrange("(k p) c -> p k c", p=P)).then_inc(blk_in[b], 16)
            sp.dma_start(w_o, I["w_out"][0].rearrange("(k p) n -> p k n", p=P)).then_inc(wo_in, 16)

            def load(e, i, s):
                gu = slot[2 * s + i][:, 0:2 * KD * FE].rearrange("p (w c) -> p w c", w=2)
                one_e = bass.ds(e, 1)
                sp.dma_start(gu[:, 0, :], I["w_gate"][0, one_e].rearrange("o (p k) f -> p (o k f)", p=P)).then_inc(slot_in[s], 16)
                sp.dma_start(gu[:, 1, :], I["w_up"][0, one_e].rearrange("o (p k) f -> p (o k f)", p=P)).then_inc(slot_in[s], 16)
                sp.dma_start(s_dn[2 * s + i], I["w_down"][0, one_e].rearrange("o (h p) n -> p (o h) n", p=P)).then_inc(slot_in[s], 16)

            sp.wait_ge(grp_done, G_FQK + 4)
            load(0, 0, 0)
            sp.wait_ge(grp_done, G_FV + 2)
            load(1, 1, 0)
            sp.wait_ge(grp_done, G_MK + 2)
            load(2, 0, 1)
            sp.wait_ge(grp_done, G_MV + 2)
            load(3, 1, 1)
            sp.wait_ge(grp_done, G_OM + 4)
            sp.wait_ge(o_ready, PAIRS)
            load(4, 0, 2)
            load(5, 1, 2)
            sp.wait_ge(base_ready, 1)

            def load_couple(q, s):
                before_q = sp.value_load(base[0:1, bass.ds(q - (NSLOT - 1), 1)], min_val=1, max_val=ITEMS_MAX)
                sp.wait_ge(down_done, before_q)
                for i in range(2):
                    load(2 * q + i, i, s)

            with sp.Fori(1, LOOPS) as g:
                for s in range(NSLOT):
                    load_couple(g * NSLOT + s, s)
            for s in range(TAIL):
                load_couple(LOOPS * NSLOT + s, s)
            for t in range(NT):
                sp.wait_ge(fin_ready, t + 1)
                sp.dma_start(out[0, t * P:(t + 1) * P, :], outb[t]).then_inc(out_done, 16)
            sp.wait_ge(out_done, 16 * NT)

        @block.tensor
        def _(pe):
            mm = nc.tensor.matmul
            pe.wait_ge(cst_in, 16)
            pe.wait_ge(gv_in, 48)
            nc.tensor.transpose(bank[0][:, 0:2 * KD], gvec, ident[0:2 * KD, 0:2 * KD]).then_inc(gcol_t, 1)
            for i in range(KD // 2):
                for t in range(NT):
                    pe.wait_ge(xn_ready, t + 1)
                    for k in (2 * i, 2 * i + 1):
                        c = (k % 2) * SEQ + t * P
                        last = nc.tensor.transpose(bank[4 + i][:, c:c + P], xn[:, t, k * P:(k + 1) * P], ident)
                last.then_inc(tr_done, 1)
            pe.wait_ge(hT_act, 1)
            pe.wait_ge(hT_dve, 1)

            def proj_major(g, w, col, width, out_cols):
                for k in range(KD):
                    last = mm(grp_bank(g)[0:width, out_cols:out_cols + SEQ], w[:, k, col:col + width], hT[:, k, :],
                              start=(k == 0), stop=(k == KD - 1))
                return last

            def proj_tokens(g, w, t):
                wait_bank_free(pe, g)
                for k in range(KD):
                    last = mm(grp_bank(g)[:, :], hT[:, k, t * P:(t + 1) * P], w[:, k, :], start=(k == 0), stop=(k == KD - 1))
                last.then_inc(grp_done, 1)

            def scores(j):
                banks = [bank[4 + 2 * (j % 2) + h] for h in range(2)]
                if j >= 2:
                    pe.wait_ge(pt_act, j - 1)
                    pe.wait_ge(pt_dve, j - 1)
                for t in range(NT):
                    nk = (t + 1) * P
                    c = t * P
                    for h in range(2):
                        mm(banks[h][:, c:c + nk], qT[HD * h:HD * (h + 1), j, t * P:(t + 1) * P],
                           kT[HD * h:HD * (h + 1), j, 0:nk], start=True, stop=False)
                    if j < FOX_PAIRS:
                        for h in range(2):
                            mm(banks[h][:, c:c + nk], neg8[:, 2 * j + h, :], cpart[:, 0:nk], start=False, stop=False)
                    for h in range(2):
                        last = mm(banks[h][:, c + t * P:c + nk], identb, causal, start=False, stop=True)
                last.then_inc(s_done, 1)

            def transposes(j):
                pe.wait_ge(p_ready, j + 1)
                for h in range(2):
                    b, p = bank[4 + 2 * (j % 2) + h], prob[j % 2][h]
                    for i in range(3):
                        last = nc.tensor.transpose(b[:, i * P:(i + 1) * P], p[:, i * P:(i + 1) * P], ident)
                last.then_inc(t_done, 1)

            def values(j):
                pe.wait_ge(pt_act, j + 1)
                pe.wait_ge(pt_dve, j + 1)
                if j >= 1:
                    pe.wait_ge(o_taken, j)
                for h in range(2):
                    mm(bank[O_BANK][HD * h:HD * (h + 1), 0:SEQ], v[:, 0, HD * (2 * j + h):HD * (2 * j + h + 1)],
                       probT[j % 2][h][:, 0:SEQ], start=True, stop=False)
                for h in range(2):
                    last = mm(bank[O_BANK][HD * h:HD * (h + 1), P:SEQ], v[:, 1, HD * (2 * j + h):HD * (2 * j + h + 1)],
                              probT[j % 2][h][:, SEQ:PW], start=False, stop=True)
                last.then_inc(o_done, 1)

            def sum_squares(g, group):
                wait_bank_free(pe, g)
                pe.wait_ge(o_ready, FOX_PAIRS * (group + 1))
                for t in range(NT):
                    last = mm(grp_bank(g)[:, t:t + 1], sqacc[:, group, t * P:(t + 1) * P], onescol, start=True, stop=True)
                last.then_inc(grp_done, 1)

            def out_proj(g, group, t, half):
                wait_bank_free(pe, g)
                for k in range(FOX_PAIRS):
                    j = FOX_PAIRS * group + k
                    last = mm(grp_bank(g)[:, :], oT[:, j, t * P:(t + 1) * P], w_o[:, j, half * HALF:(half + 1) * HALF],
                              start=(k == 0), stop=(k == FOX_PAIRS - 1))
                last.then_inc(grp_done, 1)

            pe.wait_ge(wf_in, 16)
            pe.wait_ge(gcol_set, 1)
            proj_major(G_FT, wf, 0, N_FOX, 0).then_inc(grp_done, 1)
            for w in range(2):
                pe.wait_ge(blk_in[w], 16)
                for i in range(2):
                    g = G_FQK + 2 * w + i
                    wait_bank_free(pe, g)
                    proj_major(g, w_blk[w], (2 * i) * P, P, 0)
                    proj_major(g, w_blk[w], (2 * i + 1) * P, P, SEQ).then_inc(grp_done, 1)
            pe.wait_ge(blk_in[2], 16)
            for t in range(NT):
                proj_tokens(G_FV + t, w_blk[2], t)
            pe.wait_ge(act_took, G_FV)
            pe.wait_ge(fc_ready, 1)
            pe.wait_ge(fg_in, 48)
            scores(0)
            scores(1)
            pe.wait_ge(blk_in[3], 16)
            proj_tokens(G_MQ, w_blk[3], 0)
            pe.wait_ge(act_took, G_MQ)
            transposes(0)
            transposes(1)
            proj_tokens(G_MQ + 1, w_blk[3], 1)
            values(0)
            scores(2)
            values(1)
            scores(3)
            pe.wait_ge(blk_in[4], 16)
            proj_tokens(G_MK, w_blk[4], 0)
            transposes(2)
            transposes(3)
            proj_tokens(G_MK + 1, w_blk[4], 1)
            values(2)
            values(3)
            pe.wait_ge(blk_in[5], 16)
            proj_tokens(G_MV, w_blk[5], 0)
            pe.wait_ge(rope_done, 4)
            for w in range(2):
                for i in range(FOX_PAIRS):
                    for t in range(NT):
                        c = (i % 2) * SEQ + t * P
                        last = nc.tensor.transpose(bank[4 + 2 * w + i // 2][:, c:c + P], mqk[:, w, t, i * P:(i + 1) * P], ident)
            last.then_inc(xt_done, 1)
            proj_tokens(G_MV + 1, w_blk[5], 1)
            pe.wait_ge(xt_act, 1)
            pe.wait_ge(xt_dve, 1)
            scores(4)
            scores(5)
            sum_squares(G_SF, 0)
            pe.wait_ge(wo_in, 16)
            out_proj(G_OF, 0, 0, 0)
            out_proj(G_OF + 1, 0, 0, 1)
            transposes(4)
            transposes(5)
            out_proj(G_OF + 2, 0, 1, 0)
            pe.wait_ge(act_took, G_SF)
            values(4)
            scores(6)
            values(5)
            scores(7)
            out_proj(G_OF + 3, 0, 1, 1)
            transposes(6)
            transposes(7)
            values(6)
            values(7)
            sum_squares(G_SM, 1)
            for i in range(4):
                out_proj(G_OM + i, 1, i // 2, i % 2)

            for t in range(NT):
                pe.wait_ge(h2_ready, t + 1)
                for i in range(KD // 2):
                    for k in (2 * i, 2 * i + 1):
                        c = (k % 2) * SEQ + t * P
                        last = nc.tensor.transpose(bank[4 + i][:, c:c + P], h2[:, t, k * P:(k + 1) * P], ident)
                    if t == NT - 1:
                        last.then_inc(h2t_done, 1)
            pe.wait_ge(h2T_act, 1)
            pe.wait_ge(wr_in, 32)
            for k in range(KD):
                if k == KD // 2:
                    pe.wait_ge(h2T_dve, 1)
                b = HD * (k % 2)
                last = mm(bank[4][b:b + LGP, 0:SEQ], wr[:, k, :], h2T[:, k, :], start=(k < 2), stop=(k >= KD - 2))
            last.then_inc(lgT_done, 1)
            pe.wait_ge(lgT_ready, 1)
            pe.wait_ge(add_in, 16)
            for t in range(NT):
                last = mm(bank[5][:, t * LGP:t * LGP + LG], lgT[:, t * P:(t + 1) * P], add2[:, :], start=True, stop=True)
            last.then_inc(logits_done, 1)
            pe.wait_ge(dve_took, G_OM + 4 - G_SF)
            for t in range(NT):
                for half in range(2):
                    mm(acc[t][half][:, :], ident, x[:, t, half * HALF:(half + 1) * HALF], start=True, stop=False)
            pe.wait_ge(member_ready, 1)
            mm(bank[4][:, 0:E], before, member[:, 0, :], start=True, stop=True)
            mm(bank[4][:, E:2 * E], onesb, member[:, 0, :], start=True, stop=False)
            mm(bank[4][:, E:2 * E], before, member[:, 1, :], start=False, stop=True)
            mm(bank[4][:, 2 * E:3 * E], onesb, member[:, 0, :], start=True, stop=False)
            mm(bank[4][:, 2 * E:3 * E], onesb, member[:, 1, :], start=False, stop=True).then_inc(rank_done, 1)

            def gather():
                for k in range(KD):
                    for t in range(NT):
                        for i in range(3):
                            last = mm(p_hg[:, k * CP:(k + 1) * CP], hs[:, i, t, k, :], selb[:, t, :],
                                      start=(t == 0 and i == 0), stop=(t == NT - 1 and i == 2))
                return last

            def gather_signalled():
                gather().then_inc(gathered, 1)

            def add_back(stop=False):
                for t in range(NT):
                    for half in range(2):
                        last = mm(acc[t][half][:, :], selT[CP * half:CP * (half + 1), t * P:(t + 1) * P],
                                  yb[CP * half:CP * (half + 1), :], start=False, stop=stop)
                return last

            pe.wait_ge(split_ready, 1)
            pe.wait_ge(sel_ready, 1)
            gather_signalled()

            def one_pass(i, turn, s):
                pe.wait_ge(slot_in[s], turn * 96 + 96)
                pe.wait_ge(hg_ready, i + 1)
                for k in range(KD):
                    for h in range(2):
                        for e in range(2):
                            b = CP * h + CAP * e
                            last = mm(p_gu[b:b + CAP, 0:FE], hg[:, k, CAP * e:CAP * (e + 1)], s_gu[2 * s + e][:, :, k, h, :],
                                      start=(k == 0), stop=(k == KD - 1))
                last.then_inc(gu_done, 1)
                pe.wait_ge(sel_ready, i + 2)
                gather_signalled()
                pe.wait_ge(selT_ready, i + 1)
                pe.wait_ge(selw_ready, i + 1)
                for t in range(NT):
                    nc.tensor.transpose(p_tr[:, t * P:(t + 1) * P], selw[:, t, :], ident)
                pe.wait_ge(act_ready, i + 1)
                nc.tensor.transpose(p_tr[:, 2 * P:3 * P], act_sb, ident).then_inc(actt_done, 1)
                pe.wait_ge(y_ready, i + 1)
                add_back().then_inc(added, 1)
                pe.wait_ge(actT_ready, i + 1)
                for f in range(2):
                    for h in range(2):
                        for e in range(2):
                            b = CP * h + CAP * e
                            last = mm(p_y[b:b + CAP, :], actT[:, CP * f + CAP * e:CP * f + CAP * (e + 1)],
                                      s_dn[2 * s + e][:, f, h * HALF:(h + 1) * HALF], start=(f == 0), stop=(f == 1))
                last.then_inc(down_done, 1)

            def couple(q, turn, s):
                first = pe.value_load(base[0:1, bass.ds(q, 1)], min_val=0, max_val=ITEMS_MAX)
                after = pe.value_load(base[0:1, bass.ds(q + 1, 1)], min_val=1, max_val=ITEMS_MAX)
                with pe.Fori(first, after) as i:
                    one_pass(i, turn, s)

            pe.wait_ge(base_ready, 1)
            with pe.Fori(0, LOOPS) as g:
                for s in range(NSLOT):
                    couple(g * NSLOT + s, g, s)
            for s in range(TAIL):
                couple(LOOPS * NSLOT + s, LOOPS, s)
            passes_all = pe.value_load(base[0:1, COUPLES:COUPLES + 1], min_val=COUPLES, max_val=ITEMS_MAX)
            pe.wait_ge(y_ready, passes_all + 1)
            pe.wait_ge(selT_ready, passes_all + 1)
            add_back(stop=True).then_inc(acc_done, 1)

        @block.scalar
        def _(act):
            A = nc.scalar.activation
            steps = [0]

            def step(ins):
                steps[0] += 1
                ins.then_inc(act_step, 1)
                act.wait_ge(act_step, steps[0])

            act.dma_start(cf[:, :], I["const_f32"]).then_inc(cst_in, 16)
            act.dma_start(cb[:, :], I["const_bf16"]).then_inc(fg_in, 16)
            act.dma_start(neg8, I["const_neg8"]).then_inc(fg_in, 16)
            act.dma_start(bfg, I["b_forget"][0].rearrange("(h o) -> h o", o=1)).then_inc(fg_in, 16)
            act.dma_start(add2[:, :], I["const_add2"]).then_inc(add_in, 16)

            def load_table(func):
                A(warm, onescol, func)

            def seed_rsqrt(k, t0=0, n=NT):
                act.wait_ge(var_ready, k + 1)
                A(seed[:, t0:t0 + n], var[:, t0:t0 + n], ACT.Sqrt).then_inc(seed_ready, 1)

            act.wait_ge(ones_set, 1)
            load_table(ACT.Sqrt)
            act.wait_ge(x_in, 16 * NT)
            for t in range(NT):
                last = A(xn[:, t, :], x[:, t, :], ACT.Square, accum_out=ssq[:, t:t + 1])
            last.then_inc(ssq_ready, 1)
            seed_rsqrt(0)
            act.wait_ge(gcol_t, 1)
            nc.scalar.copy(gcol[:, :], bank[0][:, 0:2 * KD]).then_inc(gcol_set, 1)
            act.wait_ge(gcol_set, 1)
            for i in range(2):
                act.wait_ge(tr_done, i + 1)
                for k in (2 * i, 2 * i + 1):
                    last = A(hT[:, k, :], bank[4 + i][:, (k % 2) * SEQ:(k % 2 + 1) * SEQ], ACT.Copy, scale=gcol[:, k:k + 1])
            last.then_inc(hT_act, 1)

            def took(g, dst, src):
                act.wait_ge(grp_done, g + 1)
                nc.scalar.copy(dst, src).then_inc(act_took, 1)

            act.wait_ge(fg_in, 48)
            act.wait_ge(grp_done, 1)
            A(fz, grp_bank(G_FT)[0:N_FOX, 0:SEQ], ACT.Identity, bias=bfg).then_inc(act_took, 1)
            act.wait_ge(fa_ready, 1)
            step(A(fl, fa, ACT.Exp, scale=-1.0))
            A(fl, fl, ACT.Ln, bias=1.0).then_inc(fl_ready, 1)
            for i in range(4):
                g = G_FQK + i
                a = (PAIRS if i >= 2 else 0) + 2 * (i % 2)
                took(g, qk[:, a:a + 2, :].rearrange("p a b -> p (a b)"), grp_bank(g)[:, :])
            for t in range(NT):
                took(G_FV + t, v[:, t, 0:FOX_W], grp_bank(G_FV + t)[:, :])

            def exps(j):
                act.wait_ge(nm_ready, j + 1)
                for h in range(2):
                    for t in range(NT):
                        c, nk = t * P, (t + 1) * P
                        last = A(prob[j % 2][h][:, c:c + nk], bank[4 + 2 * (j % 2) + h][:, c:c + nk], ACT.Exp,
                                 bias=nm[j % 2][:, 2 * h + t:2 * h + t + 1], scale=SCALE,
                                 accum_out=rs[j % 2][:, 2 * h + t:2 * h + t + 1])
                last.then_inc(exp_done, 1)

            def take_probT(j):
                act.wait_ge(t_done, j + 1)
                nc.scalar.copy(probT[j % 2][0], bank[4 + 2 * (j % 2)][:, 0:PW]).then_inc(pt_act, 1)

            def take_o(j):
                act.wait_ge(o_done, j + 1)
                nc.scalar.copy(oT[:, j, :], bank[O_BANK][:, 0:SEQ]).then_inc(o_taken, 1)

            def take_mqk(g):
                w, t = (g - G_MQ) // 2, (g - G_MQ) % 2
                took(g, mqk[:, w, t, :], grp_bank(g)[:, :])

            exps(0)
            exps(1)
            take_mqk(G_MQ)
            take_probT(0)
            take_probT(1)
            take_mqk(G_MQ + 1)
            take_o(0)
            take_o(1)
            exps(2)
            exps(3)
            take_mqk(G_MK)
            take_probT(2)
            take_probT(3)
            take_mqk(G_MK + 1)
            take_o(2)
            take_o(3)
            took(G_MV, v[:, 0, FOX_W:], grp_bank(G_MV)[:, :])
            act.wait_ge(xt_done, 1)
            for i in range(2):
                last = nc.scalar.copy(qT[:, 4 + 2 * i:6 + 2 * i, :].rearrange("p a b -> p (a b)"), bank[4 + i][:, :])
            last.then_inc(xt_act, 1)
            act.dma_start(gffn, I["norm_ffn_g"].to_broadcast([P, D])).then_inc(gffn_in, 16)
            act.wait_ge(xt_dve, 2)
            act.dma_start(wr[:, :, 0:N_GROUPS], I["w_router_group"][0].rearrange("(k p) g -> p k g", p=P)).then_inc(wr_in, 16)
            act.dma_start(wr[:, :, 8:LG], I["w_router_expert"][0].rearrange("(k p) g e -> p k (g e)", p=P)).then_inc(wr_in, 16)
            took(G_MV + 1, v[:, 1, FOX_W:], grp_bank(G_MV + 1)[:, :])
            exps(4)
            exps(5)
            seed_rsqrt(1)
            take_probT(4)
            take_probT(5)
            take_o(4)
            take_o(5)
            exps(6)
            exps(7)
            take_probT(6)
            take_probT(7)
            take_o(6)
            take_o(7)
            load_table(ACT.Sqrt)
            seed_rsqrt(2)
            act.wait_ge(grp_done, G_OM + 4)
            act.dma_start(biasb[:, 0:N_GROUPS], I["b_router_group"].to_broadcast([P, N_GROUPS])).then_inc(bias_in, 16)
            act.dma_start(biasb[:, 8:LG], I["b_router_expert"].rearrange("o g e -> o (g e)").to_broadcast([P, E])).then_inc(bias_in, 16)
            for t in range(NT):
                for half in range(2):
                    act.wait_ge(dve_took, G_OM - G_SF + 2 * t + half + 1)
                    last = A(pp[:, (2 * t + half) * HALF:(2 * t + half + 1) * HALF], x[:, t, half * HALF:(half + 1) * HALF], ACT.Square,
                             accum_out=sq4[:, 2 * t + half:2 * t + half + 1])
                last.then_inc(ssq_ready, 1)
                seed_rsqrt(3 + t, t, 1)
            load_table(ACT.Exp)
            def permuted(t):
                return h2[:, t, :].rearrange("p (c k) -> p k c", k=KD)

            for t in range(NT):
                act.wait_ge(h2_ready, t + 1)
                nc.scalar.copy(hs[:, 0, t, :, :], permuted(t)).then_inc(hi_ready, 1)
            act.wait_ge(h2t_done, 2)
            for i in range(2):
                last = nc.scalar.copy(h2T[:, 2 * i:2 * i + 2, :].rearrange("p a b -> p (a b)"), bank[4 + i][:, :])
            last.then_inc(h2T_act, 1)
            act.wait_ge(lgT_done, 1)
            nc.scalar.copy(lgT, bank[4][:, 0:SEQ]).then_inc(lgT_ready, 1)
            for t in range(NT):
                act.wait_ge(r1_ready, t + 1)
                nc.scalar.copy(hs[:, 1, t, :, :], res[:, t, :, :]).then_inc(mid_ready, 1)
            act.wait_ge(gm_ready, 1)
            for t in range(NT):
                last = A(gexp[:, t, :], lg[:, t, 0:8], ACT.Exp, bias=one[t][0], accum_out=one[t][1])
            last.then_inc(gexp_done, 1)
            act.wait_ge(ed_ready, 1)
            for t in range(NT):
                last = A(one[t][3], etop8[:, t, 1:2], ACT.Exp, bias=one[t][2])
            last.then_inc(eexp_done, 1)

            load_table(ACT.Sigmoid)
            act.wait_ge(split_ready, 1)
            act.dma_start(gfin, I["norm_final_g"].rearrange("(o d) -> o d", o=1).to_broadcast([P, D])).then_inc(gfin_in, 16)

            def one_pass(i):
                act.wait_ge(gu_done, i + 1)
                A(sig, p_gu[:, 0:P], ACT.Sigmoid).then_inc(sig_ready, 1)
                act.wait_ge(actt_done, i + 1)
                nc.scalar.copy(actT, p_tr[:, 2 * P:3 * P]).then_inc(actT_ready, 1)
                act.wait_ge(added, i + 1)
                nc.scalar.copy(selT, p_tr[:, 0:SEQ]).then_inc(selT_ready, 1)
                act.wait_ge(down_done, i + 1)
                nc.scalar.copy(yb, p_y[:, :]).then_inc(y_ready, 1)

            act.wait_ge(base_ready, 1)
            passes_all = act.value_load(base[0:1, COUPLES:COUPLES + 1], min_val=COUPLES, max_val=ITEMS_MAX)
            with act.Fori(0, passes_all) as i:
                one_pass(i)
            load_table(ACT.Sqrt)
            act.wait_ge(acc_done, 1)
            for t in range(NT):
                for half in range(2):
                    last = A(outb[t][:, half * HALF:(half + 1) * HALF], acc[t][half][:, :], ACT.Square,
                             accum_out=one[t][4 + half])
            last.then_inc(ssq_ready, 1)
            seed_rsqrt(5)

        @block.gpsimd
        def _(pool):
            steps = [0]

            def step(ins):
                steps[0] += 1
                ins.then_inc(pool_step, 1)
                pool.wait_ge(pool_step, steps[0])

            def rotate(g):
                w, t = (g - G_MQ) // 2, (g - G_MQ) % 2
                pool.wait_ge(act_took, g + 1)
                heads = mqk[:, w, t, :].rearrange("p (h c) -> p h c", h=N_MOBA)
                t1, t2 = heads[:, :, 0:ROT], heads[:, :, ROT:2 * ROT]
                cos = cf[:, C_COS + t * ROT:C_COS + (t + 1) * ROT].unsqueeze(1).to_broadcast([P, N_MOBA, ROT])
                sin = cf[:, C_SIN + t * ROT:C_SIN + (t + 1) * ROT].unsqueeze(1).to_broadcast([P, N_MOBA, ROT])
                for i, (a, b) in enumerate(((t1, cos), (t2, sin), (t2, cos), (t1, sin))):
                    last = nc.gpsimd.tensor_tensor(ropet[:, i], a, b, ALU.mult)
                step(last)
                nc.gpsimd.tensor_tensor(t1, ropet[:, 0], ropet[:, 1], ALU.subtract)
                last = nc.gpsimd.tensor_tensor(t2, ropet[:, 2], ropet[:, 3], ALU.add)
                step(last)
                pool.sem_inc(rope_done, 1)

            def square_and_scale(j):
                group = j // FOX_PAIRS
                pool.wait_ge(o_taken, j + 1)
                if j % FOX_PAIRS == 0:
                    step(nc.gpsimd.tensor_tensor(sqacc[:, group, :], oT[:, j, :], oT[:, j, :], ALU.mult))
                else:
                    step(nc.gpsimd.tensor_tensor(sqt, oT[:, j, :], oT[:, j, :], ALU.mult))
                    step(nc.gpsimd.tensor_tensor(sqacc[:, group, :], sqacc[:, group, :], sqt, ALU.add))
                nc.gpsimd.tensor_scalar(oT[:, j, :], oT[:, j, :], gcol[:, KD + j:KD + j + 1], None, ALU.mult).then_inc(o_ready, 1)

            pool.wait_ge(cst_in, 16)
            pool.wait_ge(gcol_set, 1)
            rotate(G_MQ)
            rotate(G_MQ + 1)
            square_and_scale(0)
            square_and_scale(1)
            rotate(G_MK)
            rotate(G_MK + 1)
            for j in range(2, PAIRS):
                square_and_scale(j)
            for t in range(NT):
                pool.wait_ge(hi_ready, t + 1)
                nc.gpsimd.tensor_tensor(res[:, t, :, :], h2[:, t, :].rearrange("p (c k) -> p k c", k=KD),
                                        hs[:, 0, t, :, :], ALU.subtract).then_inc(r1_ready, 1)
            for t in range(NT):
                pool.wait_ge(mid_ready, t + 1)
                last = nc.gpsimd.tensor_tensor(hs[:, 2, t, :, :], res[:, t, :, :], hs[:, 1, t, :, :], ALU.subtract)
            last.then_inc(split_ready, 1)
            pool.wait_ge(lgT_done, 1)
            nc.gpsimd.memset(selT, 0.0).then_inc(selT_ready, 1)
            nc.gpsimd.memset(yb, 0.0).then_inc(y_ready, 1)

        @block.vector
        def _(dve):
            V = nc.vector
            steps = [0]

            def step(ins):
                steps[0] += 1
                ins.then_inc(dve_step, 1)
                dve.wait_ge(dve_step, steps[0])

            V.memset(onescol, 1.0).then_inc(ones_set, 1)
            V.memset(cpart, 0.0)

            def refine_rsqrt(k, t0=0, n=NT):
                c = slice(t0, t0 + n)
                dve.wait_ge(seed_ready, k + 1)
                step(V.reciprocal(seed[:, c], seed[:, c]))
                step(V.scalar_tensor_tensor(out=rt[:, c], in0=seed[:, c], scalar=-0.5, in1=seed[:, c], op0=ALU.mult, op1=ALU.mult))
                step(V.tensor_tensor(rt[:, c], rt[:, c], var[:, c], ALU.mult))
                step(V.scalar_tensor_tensor(out=rstd[:, c], in0=rt[:, c], scalar=1.5, in1=seed[:, c], op0=ALU.add, op1=ALU.mult))

            dve.wait_ge(ssq_ready, 1)
            V.tensor_scalar(var, ssq, 1.0 / D, EPS, ALU.mult, ALU.add).then_inc(var_ready, 1)
            refine_rsqrt(0)
            for t in range(NT):
                V.tensor_scalar(xn[:, t, :], x[:, t, :], rstd[:, t:t + 1], None, ALU.mult).then_inc(xn_ready, 1)
            dve.wait_ge(gcol_set, 1)
            for i in range(2, 4):
                dve.wait_ge(tr_done, i + 1)
                for k in (2 * i, 2 * i + 1):
                    last = V.tensor_scalar(hT[:, k, :], bank[4 + i][:, (k % 2) * SEQ:(k % 2 + 1) * SEQ], gcol[:, k:k + 1], None, ALU.mult)
            last.then_inc(hT_dve, 1)
            dve.wait_ge(act_took, 1)
            V.scalar_tensor_tensor(out=fa, in0=fz, scalar=-1.0, in1=fz, op0=ALU.mult, op1=ALU.max).then_inc(fa_ready, 1)
            dve.wait_ge(fl_ready, 1)
            step(V.scalar_tensor_tensor(out=fz, in0=fz, scalar=0.0, in1=fl, op0=ALU.min, op1=ALU.subtract))
            step(V.tensor_tensor_scan(fc, fz, fz, 0.0, ALU.add, ALU.bypass))
            step(V.tensor_copy(cpart[0:N_FOX, :], fc))
            step(V.tensor_tensor(fa, fc, cpart[0:N_FOX, :], ALU.subtract))
            step(V.tensor_copy(cmid, fa))
            V.tensor_copy(cpart[32:32 + N_FOX, :], cmid)
            V.tensor_tensor(cpart[64:64 + N_FOX, :], fa, cmid, ALU.subtract).then_inc(fc_ready, 1)

            def maxima(j):
                dve.wait_ge(s_done, j + 1)
                for h in range(2):
                    for t in range(NT):
                        c, nk = t * P, (t + 1) * P
                        last = V.reduce_max(mx[j % 2][:, 2 * h + t:2 * h + t + 1], bank[4 + 2 * (j % 2) + h][:, c:c + nk], AX)
                step(last)
                V.tensor_scalar(nm[j % 2], mx[j % 2], -SCALE, None, ALU.mult).then_inc(nm_ready, 1)

            def normalise(j):
                dve.wait_ge(exp_done, j + 1)
                step(V.reciprocal(rs[j % 2], rs[j % 2]))
                for h in range(2):
                    for t in range(NT):
                        c, nk = t * P, (t + 1) * P
                        p = prob[j % 2][h][:, c:c + nk]
                        last = V.tensor_scalar(p, p, rs[j % 2][:, 2 * h + t:2 * h + t + 1], None, ALU.mult)
                last.then_inc(p_ready, 1)

            def take_probT(j):
                dve.wait_ge(t_done, j + 1)
                V.tensor_copy(probT[j % 2][1], bank[5 + 2 * (j % 2)][:, 0:PW]).then_inc(pt_dve, 1)

            def add_projection(g, t, half):
                dve.wait_ge(grp_done, g + 1)
                xs = x[:, t, half * HALF:(half + 1) * HALF]
                V.scalar_tensor_tensor(out=xs, in0=grp_bank(g)[:, :], scalar=rstd[:, t:t + 1], in1=xs,
                                       op0=ALU.mult, op1=ALU.add).then_inc(dve_took, 1)

            def group_variance(k, g):
                dve.wait_ge(grp_done, g + 1)
                V.tensor_scalar(var, grp_bank(g)[:, 0:NT], 1.0 / FOX_W, EPS, ALU.mult, ALU.add).then_inc(dve_took, 1)
                dve.wait_ge(dve_took, g - G_SF + 1)
                V.tensor_copy(var, var).then_inc(var_ready, 1)

            maxima(0)
            maxima(1)
            normalise(0)
            normalise(1)
            take_probT(0)
            take_probT(1)
            maxima(2)
            maxima(3)
            normalise(2)
            normalise(3)
            take_probT(2)
            take_probT(3)
            dve.wait_ge(xt_done, 1)
            for i in range(2):
                last = V.tensor_copy(kT[:, 4 + 2 * i:6 + 2 * i, :].rearrange("p a b -> p (a b)"), bank[6 + i][:, :])
            last.then_inc(xt_dve, 1)
            V.memset(stage[:, D:D + KD * LGP], 0.0).then_inc(xt_dve, 1)
            maxima(4)
            maxima(5)
            group_variance(1, G_SF)
            normalise(4)
            normalise(5)
            refine_rsqrt(1)
            add_projection(G_OF, 0, 0)
            add_projection(G_OF + 1, 0, 1)
            take_probT(4)
            take_probT(5)
            add_projection(G_OF + 2, 1, 0)
            maxima(6)
            maxima(7)
            normalise(6)
            normalise(7)
            add_projection(G_OF + 3, 1, 1)
            take_probT(6)
            take_probT(7)
            group_variance(2, G_SM)
            refine_rsqrt(2)
            dve.wait_ge(dve_took, 6)
            dve.wait_ge(gffn_in, 16)
            for t in range(NT):
                for half in range(2):
                    add_projection(G_OM + 2 * t + half, t, half)
                c = slice(t, t + 1)
                dve.wait_ge(ssq_ready, 2 + t)
                step(V.tensor_tensor(var[:, c], sq4[:, 2 * t:2 * t + 1], sq4[:, 2 * t + 1:2 * t + 2], ALU.add))
                V.tensor_scalar(var[:, c], var[:, c], 1.0 / D, EPS, ALU.mult, ALU.add).then_inc(var_ready, 1)
                refine_rsqrt(3 + t, t, 1)
                V.scalar_tensor_tensor(out=h2[:, t, :], in0=x[:, t, :], scalar=rstd[:, c], in1=gffn,
                                       op0=ALU.mult, op1=ALU.mult).then_inc(h2_ready, 1)
            dve.wait_ge(bias_in, 32)
            V.memset(biasb[:, N_GROUPS:8], NEG)
            dve.wait_ge(h2t_done, 4)
            for i in range(2, 4):
                last = V.tensor_copy(h2T[:, 2 * i:2 * i + 2, :].rearrange("p a b -> p (a b)"), bank[4 + i][:, :])
            last.then_inc(h2T_dve, 1)

            dve.wait_ge(logits_done, 1)
            for t in range(NT):
                last = V.tensor_tensor(lg[:, t, :], bank[5][:, t * LGP:t * LGP + LG], biasb, ALU.add)
            step(last)
            for t in range(NT):
                last = V.max(top8[:, t, :], lg[:, t, 0:8])
            step(last)
            for t in range(NT):
                last = V.tensor_scalar(one[t][0], top8[:, t, 0:1], -1.0, None, ALU.mult)
            last.then_inc(gm_ready, 1)
            for t in range(NT):
                last = V.max_index(idx8[:, t, :], top8[:, t, :], lg[:, t, 0:8])
            step(last)
            for t in range(NT):
                last = V.tensor_copy(one[t][6], idx8[:, t, 0:1])
            step(last)
            for t in range(NT):
                last = V.tensor_scalar(gmask[:, t, :], iota[:, 0:N_GROUPS], one[t][6], None, ALU.is_equal)
            step(last)
            for g in range(N_GROUPS):
                for t in range(NT):
                    e8 = lg[:, t, 8 + EPG * g:8 + EPG * (g + 1)]
                    if g == 0:
                        last = V.tensor_scalar(el8[:, t, :], e8, gmask[:, t, 0:1], None, ALU.mult)
                    else:
                        last = V.scalar_tensor_tensor(out=el8[:, t, :], in0=e8, scalar=gmask[:, t, g:g + 1], in1=el8[:, t, :],
                                                      op0=ALU.mult, op1=ALU.add)
                step(last)
            for t in range(NT):
                last = V.max(etop8[:, t, :], el8[:, t, :])
            step(last)
            for t in range(NT):
                last = V.tensor_scalar(one[t][2], etop8[:, t, 0:1], -1.0, None, ALU.mult)
            last.then_inc(ed_ready, 1)
            for t in range(NT):
                last = V.max_index(eidx8[:, t, :], etop8[:, t, :], el8[:, t, :])
            step(last)
            for t in range(NT):
                V.tensor_copy(one[t][4], eidx8[:, t, 0:1])
                last = V.tensor_copy(one[t][5], eidx8[:, t, 1:2])
            step(last)
            for t in range(NT):
                for i in (4, 5):
                    last = V.scalar_tensor_tensor(out=one[t][i], in0=one[t][6], scalar=float(EPG), in1=one[t][i],
                                                  op0=ALU.mult, op1=ALU.add)
            step(last)
            for t in range(NT):
                last = V.tensor_scalar(memf[:, t, :], iota[:, 0:E], one[t][4], None, ALU.is_equal)
            step(last)
            for t in range(NT):
                last = V.scalar_tensor_tensor(out=memf[:, t, :], in0=iota[:, 0:E], scalar=one[t][5], in1=memf[:, t, :],
                                              op0=ALU.is_equal, op1=ALU.add)
            step(last)
            step(V.tensor_copy(member[:, :, :], memf[:, :, :]))
            dve.sem_inc(member_ready, 1)
            dve.wait_ge(gexp_done, 1)
            dve.wait_ge(eexp_done, 1)
            for t in range(NT):
                last = V.tensor_scalar(one[t][7], one[t][3], 1.0, one[t][1], ALU.add, ALU.mult)
            step(last)
            for t in range(NT):
                last = V.reciprocal(one[t][7], one[t][7])
            step(last)
            for t in range(NT):
                last = V.tensor_tensor(one[t][8], one[t][7], one[t][3], ALU.mult)
            step(last)
            for t in range(NT):
                V.tensor_scalar(wgt[:, t, :], iota[:, 0:E], one[t][4], one[t][7], ALU.is_equal, ALU.mult)
                last = V.tensor_scalar((wa, wb)[t], iota[:, 0:E], one[t][5], one[t][8], ALU.is_equal, ALU.mult)
            step(last)
            for t in range(NT):
                last = V.tensor_tensor(wgt[:, t, :], wgt[:, t, :], (wa, wb)[t], ALU.add)
            step(last)
            dve.wait_ge(rank_done, 1)
            V.memset(rank[:, :, E:E + 2], 0.0)
            for t in range(NT):
                last = V.scalar_tensor_tensor(out=rank[:, t, 0:E], in0=bank[4][:, t * E:(t + 1) * E], scalar=1.0, in1=memf[:, t, :],
                                              op0=ALU.add, op1=ALU.mult)
            step(last)
            V.tensor_copy(memf[:, 0, :], bank[4][:, 2 * E:3 * E])
            step(V.tensor_scalar(rank[:, :, :], rank[:, :, :], -1.0, None, ALU.add))

            def select(at_e):
                for t in range(NT):
                    for e in range(2):
                        at = rank[:, t, at_e + e:at_e + e + 1] if isinstance(at_e, int) else rank[:, t, bass.ds(at_e + e, 1)]
                        last = V.tensor_scalar(selb[:, t, CAP * e:CAP * (e + 1)], iota[:, 0:CAP], at, None, ALU.is_equal)
                last.then_inc(sel_ready, 1)

            select(0)
            pairs2 = memf[:, 0, :].rearrange("p (q e) -> p q e", e=2)
            step(V.tensor_tensor(most, pairs2[:, :, 0], pairs2[:, :, 1], ALU.max))
            step(V.tensor_scalar(passes, most, float(CAP - 1), float(CAP), ALU.add, ALU.max))
            step(V.tensor_scalar(passes, passes, CAP.bit_length() - 1, None, ALU.logical_shift_right))
            V.memset(base[:, 0:1], 0)
            V.tensor_tensor_scan(base[:, 1:COUPLES + 1], passes, passes, 0.0, ALU.add, ALU.bypass).then_inc(base_ready, 1)

            def take_gathered(i):
                dve.wait_ge(gathered, i + 1)
                V.tensor_copy(hg[:, :, :].rearrange("p k c -> p (k c)"), p_hg[:, :]).then_inc(hg_ready, 1)

            take_gathered(0)
            steps0 = steps[0]
            STEPS = 2

            def one_pass(i, after, q):
                for t in range(NT):
                    for e in range(2):
                        last = V.tensor_scalar(selw[:, t, :].rearrange("p (h e c) -> p e h c", h=2, e=2)[:, e],
                                               iota[:, 0:CP].rearrange("p (h c) -> p h c", h=2),
                                               rank[:, t, bass.ds(2 * q + e, 1)], wgt[:, t, bass.ds(2 * q + e, 1)],
                                               ALU.is_equal, ALU.mult)
                last.then_inc(selw_ready, 1)
                dve.wait_ge(selw_ready, i + 1)
                V.tensor_scalar(rank[:, :, bass.ds(2 * q, 2)], rank[:, :, bass.ds(2 * q, 2)], -float(CAP), None,
                                ALU.add).then_inc(dve_step, 1)
                dve.wait_ge(dve_step, i * STEPS + (steps0 + 1))
                select(dve.snap(2 * (q + ((i + 1) >= after))))
                dve.wait_ge(sig_ready, i + 1)
                V.tensor_tensor(gated, p_gu[:, 0:P], sig, ALU.mult).then_inc(dve_step, 1)
                dve.wait_ge(dve_step, i * STEPS + (steps0 + 2))
                V.tensor_tensor(act_sb, p_gu[:, P:2 * P], gated, ALU.mult).then_inc(act_ready, 1)
                take_gathered(i + 1)
                dve.wait_ge(actt_done, i + 1)

            def couple(q):
                first = dve.value_load(base[0:1, bass.ds(q, 1)], min_val=0, max_val=ITEMS_MAX)
                after = dve.value_load(base[0:1, bass.ds(q + 1, 1)], min_val=1, max_val=ITEMS_MAX)
                with dve.Fori(first, after) as i:
                    one_pass(i, after, q)

            dve.wait_ge(base_ready, 1)
            with dve.Fori(0, COUPLES) as q:
                couple(q)
            passes_all = dve.value_load(base[0:1, COUPLES:COUPLES + 1], min_val=COUPLES, max_val=ITEMS_MAX)

            own = passes_all * STEPS + steps0
            dve.wait_ge(gfin_in, 16)
            dve.wait_ge(ssq_ready, 4)
            for t in range(NT):
                last = V.tensor_tensor(ssq[:, t:t + 1], one[t][4], one[t][5], ALU.add)
            last.then_inc(dve_step, 1)
            dve.wait_ge(dve_step, own + 1)
            V.tensor_scalar(var, ssq, 1.0 / D, EPS, ALU.mult, ALU.add).then_inc(var_ready, 1)
            dve.wait_ge(seed_ready, 6)
            V.reciprocal(seed, seed).then_inc(dve_step, 1)
            dve.wait_ge(dve_step, own + 2)
            V.scalar_tensor_tensor(out=rt, in0=seed, scalar=-0.5, in1=seed, op0=ALU.mult, op1=ALU.mult).then_inc(dve_step, 1)
            dve.wait_ge(dve_step, own + 3)
            V.tensor_tensor(rt, rt, var, ALU.mult).then_inc(dve_step, 1)
            dve.wait_ge(dve_step, own + 4)
            V.scalar_tensor_tensor(out=rstd, in0=rt, scalar=1.5, in1=seed, op0=ALU.add, op1=ALU.mult).then_inc(dve_step, 1)
            dve.wait_ge(dve_step, own + 5)
            for t in range(NT):
                for half in range(2):
                    c = slice(half * HALF, (half + 1) * HALF)
                    last = V.scalar_tensor_tensor(out=outb[t][:, c], in0=acc[t][half][:, :], scalar=rstd[:, t:t + 1], in1=gfin[:, c],
                                                  op0=ALU.mult, op1=ALU.mult)
                last.then_inc(fin_ready, 1)


_INS = ["x", "norm_mix_g", "w_in", "b_forget", "fox_out_g", "moba_out_g", "w_out", "norm_ffn_g", "w_router_group",
        "b_router_group", "w_router_expert", "b_router_expert", "w_gate", "w_up", "w_down", "norm_final_g"]


def constants(np, bf16):
    half = ROT
    inv = (np.float32(500000.0) ** (-np.arange(half, dtype=np.float32) / np.float32(half))).astype(np.float32)
    ang = np.arange(SEQ, dtype=np.float32)[:, None] * inv[None, :]
    f = np.zeros((P, C_END), np.float32)
    f[:, C_ID:C_ID + P] = np.eye(P)
    f[:, C_IOTA:C_IOTA + P] = np.arange(P) % CAP
    for t in range(NT):
        f[:, C_COS + t * ROT:C_COS + (t + 1) * ROT] = np.cos(ang[t * P:(t + 1) * P])
        f[:, C_SIN + t * ROT:C_SIN + (t + 1) * ROT] = np.sin(ang[t * P:(t + 1) * P])
    b = np.zeros((P, 4 * P), np.float32)
    b[:, 0:P] = np.eye(P)
    b[:, P:2 * P] = np.triu(np.full((P, P), -1e30), 1)
    b[:, 2 * P:3 * P] = np.triu(np.ones((P, P)), 1)
    b[:, 3 * P:4 * P] = 1.0
    n8 = np.zeros((96, N_FOX, P), np.float32)
    for h in range(N_FOX):
        n8[[h, 32 + h, 64 + h], h, :] = -1.0 / SCALE
    a2 = np.zeros((P, LG), np.float32)
    for c in range(LG):
        a2[[c, LGP + c], c] = 1.0
    return {"const_f32": f, "const_bf16": b.astype(bf16), "const_neg8": n8.astype(bf16), "const_add2": a2}


def kernel(**inputs):
    import numpy as np
    import concourse.bacc as bacc
    from concourse.bass_utils import run_bass_kernel_spmd

    nc = bacc.Bacc("TRN2", target_bir_lowering=False, num_devices=1)
    arrays, args = {}, {}
    given = {n: np.ascontiguousarray(inputs[n]) for n in _INS}
    given.update(constants(np, mybir.dt.np(mybir.dt.bfloat16)))
    for name, a in given.items():
        arrays[f"in_{name}_dram"] = a
        args[name] = nc.dram_tensor(f"in_{name}_dram", a.shape, mybir.dt.from_np(a.dtype), kind="ExternalInput").ap()
    out = nc.dram_tensor("out_0_dram", (1, SEQ, D), mybir.dt.float32, kind="ExternalOutput").ap()
    layer_program(nc, args, out)
    r = run_bass_kernel_spmd(nc, [arrays], core_ids=[0])
    return r.results[0]["out_0_dram"]
```

```python
import concourse.bass as bass
from concourse import mybir
from contextlib import ExitStack

P = 128
SEQ = 256
D = 1024
HD = 64
NT = SEQ // P
KD = D // P
FOX_W = 512
MOBA_W = 512
N_FOX = FOX_W // HD
N_MOBA = MOBA_W // HD
MIX_W = FOX_W + MOBA_W
PAIRS = MIX_W // P
FOX_PAIRS = FOX_W // P
ROT = HD // 8
N_GROUPS = 4
EPG = 8
E = N_GROUPS * EPG
FE = 256
EPS = 1e-6
SCALE = HD ** -0.5
HALF = 512
CAP = 32
CP = 2 * CAP
COUPLES = E // 2
PASSES_MAX = SEQ // CAP
TURN = 3
EXPERT = 3 * KD * FE
FIRST = TURN + 1
LOOPS = (COUPLES - FIRST) // TURN
assert FIRST + LOOPS * TURN == COUPLES
ITEMS_MAX = COUPLES * PASSES_MAX
LG = 8 + E
LGP = 64
NEG = -3.0e38
C_ID, C_IOTA, C_COS, C_SIN, C_END = 0, P, 2 * P, 2 * P + NT * ROT, 2 * P + 2 * NT * ROT


def layer_program(nc, I, out):
    fp32, bf16, f32r = mybir.dt.float32, mybir.dt.bfloat16, mybir.dt.float32r
    i32, u32 = mybir.dt.int32, mybir.dt.uint32
    ALU, ACT, AX = mybir.AluOpType, mybir.ActivationFunctionType, mybir.AxisListType.X
    ctx = ExitStack()
    with ctx:
        def sb(name, shape, dt=fp32):
            return ctx.enter_context(nc.sbuf_tensor(name, shape, dt))

        def sem(name):
            return ctx.enter_context(nc.semaphore(name))

        ring_at = (nc.sbuf_base + 31) // 32 * 32
        ring = sb("ring", [P, 2 * TURN * EXPERT])
        work_at = (nc.sbuf_base + 31) // 32 * 32
        work = sb("work", [P, 3 * NT * D])
        x = work[:, 2 * NT * D:].rearrange("p (t d) -> p t d", t=NT)
        hT_at = (nc.sbuf_base + 31) // 32 * 32
        hT = sb("hT", [P, KD, SEQ])
        qk = sb("qk", [P, 2 * PAIRS, SEQ])
        v = work[:, 0:NT * D].rearrange("p (t c) -> p t c", t=NT)
        stage = work[:, NT * D:2 * NT * D]
        pp = sb("pp", [P, 3072])
        cf = sb("cf", [P, C_END])
        cb = sb("cb", [P, 4 * P], bf16)
        gcol = sb("gcol", [P, 3 * KD])
        add2 = sb("add2", [P, LG])
        stats = sb("stats", [P, 47])

        ident, iota = cf[:, C_ID:C_ID + P], cf[:, C_IOTA:C_IOTA + P]
        identb, causal = cb[:, 0:P], cb[:, P:2 * P]
        before, onesb = cb[:, 2 * P:3 * P], cb[:, 3 * P:4 * P]
        qT, kT = qk[:, 0:PAIRS, :], qk[:, PAIRS:2 * PAIRS, :]
        oT = qT
        xn = pp[:, 0:NT * D].rearrange("p (t d) -> p t d", t=NT)
        WI = KD * FOX_W
        w_blk = [ring[:, b * WI:(b + 1) * WI].rearrange("p (k c) -> p k c", k=KD) for b in range(6)]
        WO = 6 * WI
        w_o = ring[:, WO:WO + KD * D].rearrange("p (k c) -> p k c", k=KD)
        mqk = ring[:, 2 * WI:2 * WI + 2 * NT * MOBA_W].rearrange("p (w t c) -> p w t c", w=2, t=NT)
        T0 = WO + KD * D
        wf = ring[:, T0:T0 + KD * N_FOX].rearrange("p (k c) -> p k c", k=KD)
        gvec = ring[0:3 * KD, T0 + 64:T0 + 64 + P]
        neg8 = ring[0:96, T0 + 192:T0 + 192 + N_FOX * P // 2].bitcast(bf16).rearrange("p (h c) -> p h c", h=N_FOX)
        cpart = ring[0:96, T0 + 704:T0 + 704 + SEQ // 2].bitcast(bf16)
        cmid = ring[0:N_FOX, T0 + 832:T0 + 832 + SEQ // 2].bitcast(bf16)
        ropet = ring[:, T0 + 1216:T0 + 1216 + 4 * N_MOBA * ROT].rearrange("p (i t h r) -> p i t h r", i=4, t=NT, h=N_MOBA // 2)
        sq = ring[:, T0 + 1472:T0 + 1472 + FOX_PAIRS * SEQ].rearrange("p (j t) -> p j t", j=FOX_PAIRS)
        bfg = ring[0:N_FOX, T0 + 2496:T0 + 2497]
        def part(name, at, n, k=KD):
            return nc.alloc_sbuf_tensor_at(name, [P, k, n], f32r, offset=at)

        h_hi, h_lo = part("h_hi", hT_at, SEQ), part("h_lo", work_at + 4 * NT * D, SEQ)
        wf_hi, wf_lo = part("wf_hi", ring_at + 4 * (T0 + 2528), N_FOX), part("wf_lo", ring_at + 4 * (T0 + 2592), N_FOX)
        UNIT = FOX_W // 2
        unit_at = [ring_at + 4 * (a + i * 2 * KD * UNIT) for a in (WO, 0) for i in range(2)]
        unit_hi = [part(f"unit_hi{i}", at, UNIT) for i, at in enumerate(unit_at)]
        unit_lo = [part(f"unit_lo{i}", at + 4 * KD * UNIT, UNIT) for i, at in enumerate(unit_at)]

        def unit_buf(u):
            return (0 if u < 4 else 2) + u % 2

        def unit_src(u):
            return w_blk[u // 2][:, :, (u % 2) * UNIT:(u % 2 + 1) * UNIT]

        def wait_split(engine, u):
            if u < 4:
                engine.wait_ge(half_lo_ready, 1)
            engine.wait_ge(w_lo_ready, u + 1)

        fz, fa = v[0:N_FOX, 0, FOX_W:FOX_W + SEQ], v[0:N_FOX, 0, FOX_W + SEQ:MIX_W]
        fc, fl = v[0:N_FOX, 1, FOX_W:FOX_W + SEQ], v[0:N_FOX, 1, FOX_W + SEQ:MIX_W]
        PW = P + SEQ
        prob = [[pp[:, (2 * s + h) * PW:(2 * s + h + 1) * PW] for h in range(2)] for s in range(2)]
        probT = [[pp[:, (4 + 2 * s + h) * PW:(5 + 2 * s + h) * PW] for h in range(2)] for s in range(2)]
        ssq, var, seed, rstd, rt = (stats[:, 2 * i:2 * i + 2] for i in range(5))
        mx = [stats[:, 10 + 4 * s:14 + 4 * s] for s in range(2)]
        nm = [stats[:, 18 + 4 * s:22 + 4 * s] for s in range(2)]
        rs = [stats[:, 26 + 4 * s:30 + 4 * s] for s in range(2)]
        onescol = stats[:, 34:35]
        sq4 = stats[:, 35:39]
        rstdf = stats[:, 40:42]
        warm = [stats[:, 42 + i:43 + i] for i in range(5)]
        h2 = v
        h2T = hT
        res = pp[:, 0:NT * D].rearrange("p (t k c) -> p t k c", t=NT, k=KD)
        qkf = qk[:, :, :].rearrange("p a b -> p (a b)")
        hs = qkf[:, 0:3 * D].bitcast(bf16).rearrange("p (i t k c) -> p i t k c", i=3, t=NT, k=KD)
        half_k = (slice(0, KD // 2), slice(KD // 2, KD))
        gffn = stage[:, 0:D]
        wr = stage[:, D:D + KD * LGP].rearrange("p (k c) -> p k c", k=KD)
        lgT = stage[:, D + KD * LGP:D + KD * LGP + SEQ]
        gfin = pp[:, 0:D]
        rtr = qkf[:, 3 * D:4 * D]
        cur = [0]

        def take(n, dt=fp32):
            cur[0] += n
            got = rtr[:, cur[0] - n:cur[0]]
            return got if dt is fp32 else got.bitcast(dt)

        lg = take(NT * LG).rearrange("p (t c) -> p t c", t=NT)
        biasb = take(LG)
        rank = take(NT * (E + 2)).rearrange("p (t e) -> p t e", t=NT)
        wgt = take(NT * (E + 2)).rearrange("p (t e) -> p t e", t=NT)
        member = take(NT * E // 2, bf16).rearrange("p (t e) -> p t e", t=NT)
        memf = take(NT * E).rearrange("p (t e) -> p t e", t=NT)
        is1, is2 = (take(NT * E).rearrange("p (t e) -> p t e", t=NT) for _ in range(2))
        top8 = take(NT * 8).rearrange("p (t c) -> p t c", t=NT)
        idx8 = take(NT * 8, u32).rearrange("p (t c) -> p t c", t=NT)
        etop8 = take(NT * 8).rearrange("p (t c) -> p t c", t=NT)
        eidx8 = take(NT * 8, u32).rearrange("p (t c) -> p t c", t=NT)
        el8 = take(NT * 8).rearrange("p (t c) -> p t c", t=NT)
        gexp = take(NT * 8).rearrange("p (t c) -> p t c", t=NT)
        gmask = take(NT * N_GROUPS).rearrange("p (t c) -> p t c", t=NT)
        neg_gtop, gsum, gidx, neg_etop, eratio = (take(NT) for _ in range(5))
        expert = take(NT * 2).rearrange("p (t i) -> p t i", t=NT)
        ew = take(NT * 2).rearrange("p (t i) -> p t i", t=NT)
        ssq4 = take(NT * 2).rearrange("p (t h) -> p t h", t=NT)
        emask = take(NT * E).rearrange("p (t g e) -> p t g e", t=NT, g=N_GROUPS)
        totals = take(E)
        most, passes = take(COUPLES), take(COUPLES, i32)
        base = take(COUPLES + 1, i32)
        hTf = hT[:, :, :].rearrange("p a b -> p (a b)")
        hg = hTf[:, 0:HALF].rearrange("p (k c) -> p k c", k=KD)
        yb = [nc.alloc_sbuf_tensor_at(f"yb{h}", [P, HALF], f32r, offset=hT_at + 4 * a)
              for h, a in enumerate((HALF, 2 * HALF + SEQ))]
        selT = nc.alloc_sbuf_tensor_at("selT", [P, SEQ], f32r, offset=hT_at + 4 * 2 * HALF)
        M0 = NT * D
        selw = pp[:, M0:M0 + NT * P].rearrange("p (t c) -> p t c", t=NT)
        selb = pp[:, M0 + 256:M0 + 320].bitcast(bf16).rearrange("p (t c) -> p t c", t=NT)
        act_sb = pp[:, M0 + 320:M0 + 448]
        sig, gated = pp[:, M0 + 448:M0 + 576], pp[:, M0 + 576:M0 + 704]
        actT = pp[:, M0 + 704:M0 + 832]
        selo = pp[:, M0 + 832:M0 + 960].bitcast(bf16).rearrange("p (t c) -> p t c", t=NT)
        wcol = pp[:, M0 + 960:M0 + 961]
        place = [ring[:, s * EXPERT:(s + 1) * EXPERT] for s in range(2 * TURN)] + [work[:, :]]
        EXTRA = 2 * TURN
        w_gu = [s[:, 0:2 * KD * FE].rearrange("p (w k h f) -> p w k h f", w=2, k=KD, h=2) for s in place]
        w_dn = [s[:, 2 * KD * FE:].rearrange("p (h n) -> p h n", h=2) for s in place]

        def places(q):
            if q < TURN:
                return 2 * q, 2 * q + 1
            return (EXTRA if q == TURN else 2 * ((q - 1) % TURN)), 2 * (q % TURN) + 1

        outb = [x[:, t, :] for t in range(NT)]

        bank = [ctx.enter_context(nc.psum_tensor(f"bank{i}", [P, HALF], fp32)) for i in range(8)]
        O_BANK = 3
        acc = [[bank[0], bank[1]], [bank[2], bank[3]]]
        p_hg, p_gu, p_tr, p_y = bank[4], bank[5], bank[6], bank[7]

        x_in = [sem(f"x_in{t}") for t in range(NT)]
        cst_in, wf_in, wo_in, gv_in, wr_in = (sem(n) for n in ("cst_in", "wf_in", "wo_in", "gv_in", "wr_in"))
        fg_in, gffn_in, bias_in, gfin_in, add_in = (sem(n) for n in ("fg_in", "gffn_in", "bias_in", "gfin_in", "add_in"))
        unit_in = [sem(f"unit_in{u}") for u in range(2)]
        blk_in = [sem(f"blk_in{b}") for b in range(6)]
        gate_in = [sem(f"gate_in{p}") for p in range(EXTRA + 1)]
        up_in = [sem(f"up_in{p}") for p in range(EXTRA + 1)]
        dn_in = [sem(f"dn_in{p}") for p in range(EXTRA + 1)]
        out_done = sem("out_done")
        pool_step, dve_step, act_step = sem("pool_step"), sem("dve_step"), sem("act_step")
        ones_set, gcol_t, gcol_set = sem("ones_set"), sem("gcol_t"), sem("gcol_set")
        ssq_ready, var_ready, seed_ready, xn_ready = (sem(n) for n in ("ssq_ready", "var_ready", "seed_ready", "xn_ready"))
        tr_done, h_hi_ready, h_lo_ready = sem("tr_done"), sem("h_hi_ready"), sem("h_lo_ready")
        w_hi_ready, w_lo_ready, wf_hi_ready, wf_lo_ready = (sem(n) for n in ("w_hi_ready", "w_lo_ready", "wf_hi_ready", "wf_lo_ready"))
        pad_clear = sem("pad_clear")
        grp_done, act_took, dve_took = sem("grp_done"), sem("act_took"), sem("dve_took")
        ft_done, ss_done, sq_ready, half_lo_ready = (sem(n) for n in ("ft_done", "ss_done", "sq_ready", "half_lo_ready"))
        fz_ready, fa_ready, fl_ready, fc_ready = (sem(n) for n in ("fz_ready", "fa_ready", "fl_ready", "fc_ready"))
        s_done, nm_ready, exp_done, p_ready, t_done = (sem(n) for n in ("s_done", "nm_ready", "exp_done", "p_ready", "t_done"))
        pt_act, pt_dve, o_done, o_taken, o_ready = (sem(n) for n in ("pt_act", "pt_dve", "o_done", "o_taken", "o_ready"))
        rope_done, xt_done, xt_act, xt_dve = (sem(n) for n in ("rope_done", "xt_done", "xt_act", "xt_dve"))
        h2_ready, x2t_done, lgT_done, lgT_ready = (sem(n) for n in ("h2_ready", "x2t_done", "lgT_done", "lgT_ready"))
        h2T_act, h2T_dve, logits_done = sem("h2T_act"), sem("h2T_dve"), sem("logits_done")
        gm_ready, gexp_done, ed_ready, eexp_done = (sem(n) for n in ("gm_ready", "gexp_done", "ed_ready", "eexp_done"))
        member_ready, rank_done, base_ready = sem("member_ready"), sem("rank_done"), sem("base_ready")
        hi_ready, r1_ready, mid_ready, split_ready = (sem(n) for n in ("hi_ready", "r1_ready", "mid_ready", "split_ready"))
        gate_done = sem("gate_done")
        hg_ready, gu_done, sig_ready, sel_ready, selw_ready = (
            sem(n) for n in ("hg_ready", "gu_done", "sig_ready", "sel_ready", "selw_ready"))
        gathered, selT_ready, act_ready, actt_done = (sem(n) for n in ("gathered", "selT_ready", "act_ready", "actt_done"))
        actT_ready, down_done, y_hi_ready, y_ready, added = (
            sem(n) for n in ("actT_ready", "down_done", "y_hi_ready", "y_ready", "added"))
        wcol_ready = sem("wcol_ready")
        acc_set, acc_done, fin_ready = sem("acc_set"), sem("acc_done"), sem("fin_ready")
        rstd_ready, scaled, pool_fin_ready = sem("rstd_ready"), sem("scaled"), sem("pool_fin_ready")

        G_FQK, G_FV, G_MQ, G_MK, G_MV, G_OF, G_OM = 0, 4, 6, 8, 10, 12, 16

        def grp_bank(g):
            return bank[g % 3]

        def wait_bank_free(pe, g):
            if g >= 3:
                if g - 3 < G_OF:
                    pe.wait_ge(act_took, g - 2)
                else:
                    pe.wait_ge(dve_took, g - 3 - G_OF + 1)

        LATE = PAIRS - 2

        block = ctx.enter_context(nc.Block())

        @block.sync
        def _(sp):
            for t in range(NT):
                sp.dma_start(x[:, t, :], I["x"][0, t * P:(t + 1) * P, :]).then_inc(x_in[t], 16)
            sp.dma_start(gvec[0:KD, :], I["norm_mix_g"][0].rearrange("(k p) -> k p", p=P)).then_inc(gv_in, 16)
            sp.dma_start(gvec[KD:KD + 4, :], I["fox_out_g"][0].rearrange("(k p) -> k p", p=P)).then_inc(gv_in, 16)
            sp.dma_start(gvec[KD + 4:2 * KD, :], I["moba_out_g"][0].rearrange("(k p) -> k p", p=P)).then_inc(gv_in, 16)
            sp.dma_start(gvec[2 * KD:3 * KD, :], I["norm_ffn_g"][0].rearrange("(k p) -> k p", p=P)).then_inc(gv_in, 16)
            sp.dma_start(wf, I["w_in"][0, :, 3 * FOX_W:3 * FOX_W + N_FOX].rearrange("(k p) c -> p k c", p=P)).then_inc(wf_in, 16)
            for b in range(6):
                c0 = b * FOX_W + (N_FOX if b >= 3 else 0)
                if b == 0:
                    for u in range(2):
                        sp.dma_start(unit_src(u), I["w_in"][0, :, u * UNIT:(u + 1) * UNIT].rearrange("(k p) c -> p k c", p=P)).then_inc(unit_in[u], 16)
                else:
                    if b == 1:
                        sp.dma_start(cb[:, :], I["const_bf16"]).then_inc(fg_in, 16)
                        sp.dma_start(neg8, I["const_neg8"]).then_inc(fg_in, 16)
                        sp.dma_start(bfg, I["b_forget"][0].rearrange("(h o) -> h o", o=1)).then_inc(fg_in, 16)
                        sp.dma_start(add2[:, :], I["const_add2"]).then_inc(add_in, 16)
                    sp.dma_start(w_blk[b], I["w_in"][0, :, c0:c0 + FOX_W].rearrange("(k p) c -> p k c", p=P)).then_inc(blk_in[b], 16)
            sp.wait_ge(grp_done, 4)
            sp.dma_start(w_o, I["w_out"][0].rearrange("(k p) n -> p k n", p=P)).then_inc(wo_in, 16)

            def load_half(e, p, w):
                gu = place[p][:, 0:2 * KD * FE].rearrange("p (w c) -> p w c", w=2)
                src = I[("w_gate", "w_up")[w]][0, bass.ds(e, 1)]
                sp.dma_start(gu[:, w, :], src.rearrange("o (p k) f -> p (o k f)", p=P)).then_inc((gate_in, up_in)[w][p], 16)

            def load_gu(e, p):
                load_half(e, p, 0)
                load_half(e, p, 1)

            def load_dn(e, p):
                sp.dma_start(w_dn[p], I["w_down"][0, bass.ds(e, 1)].rearrange("o (h p) n -> p (o h) n", p=P)).then_inc(dn_in[p], 16)

            def load(e):
                load_gu(e, e)
                load_dn(e, e)

            sp.wait_ge(w_lo_ready, 10)
            load(2)
            sp.wait_ge(w_lo_ready, 12)
            load(3)
            sp.wait_ge(grp_done, G_OF)
            load(0)
            sp.wait_ge(xt_done, 1)
            load(1)
            sp.wait_ge(grp_done, G_OF + 4)
            load_gu(4, 4)
            sp.wait_ge(ss_done, 2)
            load_half(5, 5, 1)
            load_dn(5, 5)
            sp.wait_ge(grp_done, G_OM + 4)
            load_half(5, 5, 0)
            load_dn(4, 4)
            sp.wait_ge(h2_ready, 3)
            sp.wait_ge(logits_done, NT)
            load_half(2 * TURN, EXTRA, 1)
            sp.wait_ge(acc_set, 1)
            load_dn(2 * TURN, EXTRA)
            sp.wait_ge(r1_ready, 3)
            load_half(2 * TURN, EXTRA, 0)
            sp.wait_ge(base_ready, 1)

            def refill(after_q, loads):
                passed = sp.value_load(base[0:1, bass.ds(after_q + 1, 1)], min_val=1, max_val=ITEMS_MAX)
                for w, used in enumerate((gate_done, gu_done)):
                    sp.wait_ge(used, passed)
                    for e, p in loads:
                        load_half(e, p, w)
                sp.wait_ge(down_done, passed)
                for e, p in loads:
                    load_dn(e, p)

            for q in range(TURN):
                refill(q, ((2 * (q + TURN) + 1, places(q + TURN)[1]), (2 * (q + FIRST), places(q + FIRST)[0])))
            q = FIRST + TURN - 1
            refill(TURN, ((2 * q + 1, places(q)[1]),))
            with sp.Fori(1, LOOPS) as g:
                for j in range(TURN):
                    refill(g * TURN + (FIRST - TURN + j), [(2 * (g * TURN + (FIRST + j)) + i, places(FIRST + j)[i]) for i in range(2)])
            for t in range(NT):
                for half in range(2):
                    h = slice(half * HALF, (half + 1) * HALF)
                    if (t, half) == (1, 1):
                        sp.wait_ge(pool_fin_ready, 1)
                    else:
                        sp.wait_ge(fin_ready, 2 * t + half + 1)
                    sp.dma_start(out[0, t * P:(t + 1) * P, h], outb[t][:, h]).then_inc(out_done, 16)
            sp.wait_ge(out_done, 16 * 2 * NT)

        @block.tensor
        def _(pe):
            mm = nc.tensor.matmul
            pe.wait_ge(cst_in, 16)
            pe.wait_ge(gv_in, 64)
            nc.tensor.transpose(bank[0][:, 0:3 * KD], gvec, ident[0:3 * KD, 0:3 * KD]).then_inc(gcol_t, 1)
            for t in range(NT):
                pe.wait_ge(xn_ready, t + 1)
                for i in range(KD // 2):
                    for k in (2 * i, 2 * i + 1):
                        c = (k % 2) * SEQ + t * P
                        last = nc.tensor.transpose(bank[4 + i][:, c:c + P], xn[:, t, k * P:(k + 1) * P], ident)
                    if t == NT - 1:
                        last.then_inc(tr_done, 1)
            def unit(u, parts=(0, 1)):
                if parts[0] == 0:
                    wait_bank_free(pe, u)
                    pe.wait_ge(w_hi_ready, u + 1)
                hi, lo = unit_hi[unit_buf(u)], unit_lo[unit_buf(u)]
                for i in parts:
                    out = grp_bank(u)[:, i * UNIT:(i + 1) * UNIT]
                    if u < G_FV:
                        for n, (w, h) in enumerate(((hi, h_hi), (hi, h_lo), (lo, h_hi))):
                            if n == 2:
                                wait_split(pe, u)
                            for k in range(KD):
                                if u == 0 and i == 0 and n < 2:
                                    pe.wait_ge((h_hi_ready, h_lo_ready)[n], k + 1)
                                last = mm(out, w[:, k, i * P:(i + 1) * P], h[:, k, :], start=(n == 0 and k == 0), stop=(n == 2 and k == KD - 1))
                    else:
                        for n, (h, w) in enumerate(((h_hi, hi), (h_lo, hi), (h_hi, lo))):
                            if n == 2:
                                wait_split(pe, u)
                            for k in range(KD):
                                last = mm(out, h[:, k, i * P:(i + 1) * P], w[:, k, :], start=(n == 0 and k == 0), stop=(n == 2 and k == KD - 1))
                if parts[-1] == 1:
                    last.then_inc(grp_done, 1)

            def scores(j):
                banks = [bank[4 + 2 * (j % 2) + h] for h in range(2)]
                if j >= 2:
                    pe.wait_ge(pt_act, j - 1)
                    pe.wait_ge(pt_dve, j - 1)
                for t in range(NT):
                    nk = (t + 1) * P
                    c = t * P
                    for h in range(2):
                        mm(banks[h][:, c:c + nk], qT[HD * h:HD * (h + 1), j, t * P:(t + 1) * P],
                           kT[HD * h:HD * (h + 1), j, 0:nk], start=True, stop=False)
                    if j < FOX_PAIRS:
                        for h in range(2):
                            mm(banks[h][:, c:c + nk], neg8[:, 2 * j + h, :], cpart[:, 0:nk], start=False, stop=False)
                    for h in range(2):
                        last = mm(banks[h][:, c + t * P:c + nk], identb, causal, start=False, stop=True)
                last.then_inc(s_done, 1)

            def transposes(j):
                pe.wait_ge(p_ready, j + 1)
                for h in range(2):
                    b, p = bank[4 + 2 * (j % 2) + h], prob[j % 2][h]
                    for i in range(3):
                        last = nc.tensor.transpose(b[:, i * P:(i + 1) * P], p[:, i * P:(i + 1) * P], ident)
                last.then_inc(t_done, 1)

            def values(j):
                pe.wait_ge(pt_act, j + 1)
                pe.wait_ge(pt_dve, j + 1)
                if j >= 1:
                    pe.wait_ge(o_taken, j)
                for h in range(2):
                    mm(bank[O_BANK][HD * h:HD * (h + 1), 0:SEQ], v[:, 0, HD * (2 * j + h):HD * (2 * j + h + 1)],
                       probT[j % 2][h][:, 0:SEQ], start=True, stop=False)
                for h in range(2):
                    last = mm(bank[O_BANK][HD * h:HD * (h + 1), P:SEQ], v[:, 1, HD * (2 * j + h):HD * (2 * j + h + 1)],
                              probT[j % 2][h][:, SEQ:PW], start=False, stop=True)
                last.then_inc(o_done, 1)

            def sum_squares(group):
                pe.wait_ge(o_taken, FOX_PAIRS * (group + 1))
                pe.wait_ge(sq_ready, group + 1)
                for t in range(NT):
                    last = mm(bank[O_BANK][:, SEQ + t:SEQ + t + 1], sq[:, 0, t * P:(t + 1) * P], onescol, start=True, stop=True)
                last.then_inc(ss_done, 1)

            def out_proj(g, t, half, k0=0, k1=FOX_PAIRS):
                group = (g - G_OF) // 4
                if k0 == 0:
                    wait_bank_free(pe, g)
                for k in range(k0, k1):
                    j = FOX_PAIRS * group + k
                    if j >= LATE:
                        pe.wait_ge(o_taken, j + 1)
                    else:
                        pe.wait_ge(o_ready, j + 1)
                    last = mm(grp_bank(g)[:, :], oT[:, j, t * P:(t + 1) * P], w_o[:, j, half * HALF:(half + 1) * HALF],
                              start=(k == 0), stop=(k == FOX_PAIRS - 1))
                if k1 == FOX_PAIRS:
                    last.then_inc(grp_done, 1)

            pe.wait_ge(gcol_set, 1)
            unit(0)
            unit(1)
            pe.wait_ge(wf_lo_ready, 1)
            for n, (w, h) in enumerate(((wf_hi, h_hi), (wf_hi, h_lo), (wf_lo, h_hi))):
                for k in range(KD):
                    last = mm(bank[O_BANK][0:N_FOX, 0:SEQ], w[:, k, :], h[:, k, :], start=(n == 0 and k == 0), stop=(n == 2 and k == KD - 1))
            last.then_inc(ft_done, 1)
            unit(2)
            unit(3)
            unit(4)
            pe.wait_ge(act_took, G_FV)
            pe.wait_ge(fc_ready, 1)
            pe.wait_ge(fg_in, 48)
            scores(0)
            scores(1)
            unit(5)
            unit(6)
            pe.wait_ge(act_took, G_MQ)
            transposes(0)
            transposes(1)
            unit(7)
            values(0)
            scores(2)
            values(1)
            scores(3)
            unit(8)
            unit(9)
            transposes(2)
            transposes(3)
            unit(10)
            values(2)
            values(3)
            pe.wait_ge(rope_done, 4)
            for w in range(2):
                for i in range(FOX_PAIRS):
                    for t in range(NT):
                        c = (i % 2) * SEQ + t * P
                        last = nc.tensor.transpose(bank[4 + 2 * w + i // 2][:, c:c + P], mqk[:, w, t, i * P:(i + 1) * P], ident)
            last.then_inc(xt_done, 1)
            unit(11, (0,))
            pe.wait_ge(xt_act, 1)
            pe.wait_ge(xt_dve, 1)
            scores(4)
            scores(5)
            unit(11, (1,))
            sum_squares(0)
            pe.wait_ge(wo_in, 16)
            out_proj(G_OF, 0, 0)
            transposes(4)
            transposes(5)
            out_proj(G_OF + 1, 0, 1, 0, 2)
            pe.wait_ge(act_took, G_OF)
            pe.wait_ge(var_ready, 3)
            values(4)
            scores(6)
            values(5)
            scores(7)
            out_proj(G_OF + 1, 0, 1, 2, 4)
            out_proj(G_OF + 2, 1, 0)
            transposes(6)
            out_proj(G_OF + 3, 1, 1, 0, 2)
            transposes(7)
            out_proj(G_OF + 3, 1, 1, 2, 4)
            values(6)
            values(7)
            out_proj(G_OM, 0, 0)
            sum_squares(1)
            out_proj(G_OM + 1, 0, 1)
            out_proj(G_OM + 2, 1, 0)

            def transpose_x(t, tiles, b):
                for i, k in enumerate(tiles):
                    last = nc.tensor.transpose(bank[b][:, i * P:(i + 1) * P], x[:, t, k * P:(k + 1) * P], ident)
                last.then_inc(x2t_done, 1)

            def router_logits(t, tiles):
                for k in tiles:
                    b = LGP * (k % 2)
                    last = mm(bank[O_BANK][b:b + LGP, t * P:(t + 1) * P], wr[:, k, :], h2T[:, k, t * P:(t + 1) * P],
                              start=(k < 2), stop=(k >= KD - 2))
                    if k == KD - 1:
                        last.then_inc(lgT_done, 1)

            def sum_logits(t):
                pe.wait_ge(lgT_ready, t + 1)
                mm(bank[5][:, t * LGP:t * LGP + LG], lgT[:, t * P:(t + 1) * P], add2[:, :], start=True, stop=True).then_inc(logits_done, 1)

            def start_acc(t, half):
                return mm(acc[t][half][:, :], ident, x[:, t, half * HALF:(half + 1) * HALF], start=True, stop=False)

            pe.wait_ge(dve_took, G_OM - G_OF + 2)
            transpose_x(0, range(0, 4), 4)
            transpose_x(0, range(4, 8), 5)
            out_proj(G_OM + 3, 1, 1, 0, 2)
            pe.wait_ge(wr_in, 32)
            pe.wait_ge(h2T_act, 1)
            router_logits(0, range(0, 4))
            pe.wait_ge(h2T_dve, 1)
            router_logits(0, range(4, 8))
            pe.wait_ge(dve_took, G_OM - G_OF + 3)
            transpose_x(1, range(0, 4), 6)
            out_proj(G_OM + 3, 1, 1, 2, 4)
            pe.wait_ge(add_in, 16)
            sum_logits(0)
            pe.wait_ge(h2T_act, 2)
            router_logits(1, range(0, 4))
            pe.wait_ge(dve_took, G_OM - G_OF + 4)
            transpose_x(1, (4, 5), 7)
            transpose_x(1, (6, 7), 4)
            start_acc(0, 0)
            pe.wait_ge(h2T_dve, 2)
            router_logits(1, (4, 5))
            pe.wait_ge(h2T_act, 3)
            router_logits(1, (6, 7))
            start_acc(0, 1)
            sum_logits(1)
            start_acc(1, 0)
            start_acc(1, 1).then_inc(acc_set, 1)
            pe.wait_ge(member_ready, 1)
            mm(bank[4][:, 0:E], before, member[:, 0, :], start=True, stop=True)
            mm(bank[4][:, E:2 * E], onesb, member[:, 0, :], start=True, stop=False)
            mm(bank[4][:, E:2 * E], before, member[:, 1, :], start=False, stop=True)
            mm(bank[4][:, 2 * E:3 * E], onesb, member[:, 0, :], start=True, stop=False)
            mm(bank[4][:, 2 * E:3 * E], onesb, member[:, 1, :], start=False, stop=True).then_inc(rank_done, 1)

            def gather(first=False):
                for k in range(KD):
                    if first and k % (KD // 2) == 0:
                        pe.wait_ge(split_ready, 1 + k // (KD // 2))
                    for t in range(NT):
                        for i in range(3):
                            last = mm(p_hg[:, k * CP:(k + 1) * CP], hs[:, i, t, k, :], selb[:, t, :],
                                      start=(t == 0 and i == 0), stop=(t == NT - 1 and i == 2))
                return last

            def gather_signalled():
                gather().then_inc(gathered, 1)

            def add_back(half, final=False):
                for t in range(NT):
                    last = mm(acc[t][half][:, :], selT[:, t * P:(t + 1) * P], yb[half][:, :], start=False, stop=final)
                    if final:
                        last.then_inc(acc_done, 1)
                return last

            pe.wait_ge(sel_ready, 1)
            gather(first=True).then_inc(gathered, 1)

            def add_result(i):
                pe.wait_ge(y_ready, 2 * i + 1)
                add_back(0)
                pe.wait_ge(y_ready, 2 * i + 2)
                add_back(1).then_inc(added, 1)

            def one_pass(i, at, loaded):
                pe.wait_ge(hg_ready, i + 1)
                for w in range(2):
                    for e in range(2):
                        pe.wait_ge((gate_in, up_in)[w][at[e]], loaded[e] * 16)
                    for k in range(KD):
                        for h in range(2):
                            for e in range(2):
                                b = CP * h + CAP * e
                                last = mm(p_gu[b:b + CAP, w * P:(w + 1) * P], hg[:, k, CAP * e:CAP * (e + 1)], w_gu[at[e]][:, w, k, h, :],
                                          start=(k == 0), stop=(k == KD - 1))
                    last.then_inc((gate_done, gu_done)[w], 1)
                pe.wait_ge(sel_ready, i + 2)
                gather_signalled()
                pe.wait_ge(selT_ready, i + 1)
                pe.wait_ge(selw_ready, i + 1)
                for t in range(NT):
                    mm(p_tr[:, t * P:(t + 1) * P], selo[:, t, :], identb, start=True, stop=True)
                for t in range(NT):
                    mm(p_tr[:, 3 * P:3 * P + 1], selw[:, t, :], onescol, start=(t == 0), stop=(t == NT - 1))
                pe.wait_ge(act_ready, i + 1)
                nc.tensor.transpose(p_tr[:, 2 * P:3 * P], act_sb, ident).then_inc(actt_done, 1)
                add_result(i)
                pe.wait_ge(actT_ready, i + 1)
                for e in range(2):
                    pe.wait_ge(dn_in[at[e]], loaded[e] * 16)
                for f in range(2):
                    for h in range(2):
                        for e in range(2):
                            b = CP * h + CAP * e
                            last = mm(p_y[b:b + CAP, :], actT[:, CP * f + CAP * e:CP * f + CAP * (e + 1)],
                                      w_dn[at[e]][:, f, h * HALF:(h + 1) * HALF], start=(f == 0), stop=(f == 1))
                last.then_inc(down_done, 1)

            def couple(q, at, loaded):
                first = pe.value_load(base[0:1, bass.ds(q, 1)], min_val=0, max_val=ITEMS_MAX)
                after = pe.value_load(base[0:1, bass.ds(q + 1, 1)], min_val=1, max_val=ITEMS_MAX)
                with pe.Fori(first, after) as i:
                    one_pass(i, at, loaded)

            pe.wait_ge(base_ready, 1)
            for q in range(TURN):
                couple(q, places(q), (1, 1))
            couple(TURN, places(TURN), (1, 2))
            with pe.Fori(0, LOOPS) as g:
                for j in range(TURN):
                    couple(g * TURN + (FIRST + j), places(FIRST + j), (g + 2, g + (3 if j == TURN - 1 else 2)))
            passes_all = pe.value_load(base[0:1, COUPLES:COUPLES + 1], min_val=COUPLES, max_val=ITEMS_MAX)
            pe.wait_ge(selT_ready, passes_all + 1)
            for half in range(2):
                pe.wait_ge(y_ready, passes_all * 2 + (half + 1))
                add_back(half, final=True)

        @block.scalar
        def _(act):
            A = nc.scalar.activation
            steps = [0]

            def step(ins):
                steps[0] += 1
                ins.then_inc(act_step, 1)
                act.wait_ge(act_step, steps[0])

            def load_table(func):
                A(warm.pop(), onescol, func)

            def seed_rsqrt(k, t0=0, n=NT):
                act.wait_ge(var_ready, k + 1)
                A(seed[:, t0:t0 + n], var[:, t0:t0 + n], ACT.Sqrt).then_inc(seed_ready, 1)

            act.wait_ge(ones_set, 1)
            load_table(ACT.Sqrt)
            act.dma_start(cf[:, :], I["const_f32"]).then_inc(cst_in, 16)
            for t in range(NT):
                act.wait_ge(x_in[t], 16)
                A(xn[:, t, :], x[:, t, :], ACT.Square, accum_out=ssq[:, t:t + 1]).then_inc(ssq_ready, 1)
                seed_rsqrt(t, t, 1)
            act.wait_ge(gcol_t, 1)
            nc.scalar.copy(gcol[:, :], bank[0][:, 0:3 * KD]).then_inc(gcol_set, 1)
            act.wait_ge(gcol_set, 1)

            def took(g, dst, src):
                act.wait_ge(grp_done, g + 1)
                nc.scalar.copy(dst, src).then_inc(act_took, 1)

            def wait_unit_in(u):
                if u < 2:
                    act.wait_ge(unit_in[u], 16)
                else:
                    act.wait_ge(blk_in[u // 2], 16)

            def split_hi(u):
                wait_unit_in(u)
                if u in (4, 5):
                    wait_split(act, 2 * (u - 4) + 1)
                elif u >= 2:
                    act.wait_ge(grp_done, u - 1)
                nc.scalar.copy(unit_hi[unit_buf(u)][:, :, :], unit_src(u)).then_inc(w_hi_ready, 1)

            def take_qk(g):
                a = (PAIRS if g >= 2 else 0) + 2 * (g % 2)
                took(g, qk[:, a:a + 2, :].rearrange("p a b -> p (a b)"), grp_bank(g)[:, :])

            def both_tiles(g):
                return grp_bank(g)[:, :].rearrange("p (t c) -> p t c", t=NT)

            def take_v(g):
                c = (0 if g < G_MQ else FOX_W) + (g % 2) * UNIT
                took(g, v[:, :, c:c + UNIT], both_tiles(g))

            def take_mqk(g):
                w, c = (g - G_MQ) // 2, (g % 2) * UNIT
                took(g, mqk[:, w, :, c:c + UNIT], both_tiles(g))

            for k in range(KD):
                if k == KD // 2:
                    split_hi(0)
                act.wait_ge(tr_done, k // 2 + 1)
                A(h_hi[:, k, :], bank[4 + k // 2][:, (k % 2) * SEQ:(k % 2 + 1) * SEQ], ACT.Copy, scale=gcol[:, k:k + 1]).then_inc(h_hi_ready, 1)
            split_hi(1)
            act.wait_ge(wf_in, 16)
            nc.scalar.copy(wf_hi[:, :, :], wf).then_inc(wf_hi_ready, 1)
            take_qk(0)
            split_hi(2)
            take_qk(1)
            split_hi(3)
            split_hi(4)
            act.wait_ge(fg_in, 48)
            act.wait_ge(ft_done, 1)
            A(fz, bank[O_BANK][0:N_FOX, 0:SEQ], ACT.Identity, bias=bfg).then_inc(fz_ready, 1)
            act.wait_ge(fa_ready, 1)
            step(A(fl, fa, ACT.Exp, scale=-1.0))
            A(fl, fl, ACT.Ln, bias=1.0).then_inc(fl_ready, 1)
            take_qk(2)
            split_hi(5)
            take_qk(3)
            take_v(4)
            split_hi(6)

            def exps(j):
                act.wait_ge(nm_ready, j + 1)
                for h in range(2):
                    for t in range(NT):
                        c, nk = t * P, (t + 1) * P
                        last = A(prob[j % 2][h][:, c:c + nk], bank[4 + 2 * (j % 2) + h][:, c:c + nk], ACT.Exp,
                                 bias=nm[j % 2][:, 2 * h + t:2 * h + t + 1], scale=SCALE,
                                 accum_out=rs[j % 2][:, 2 * h + t:2 * h + t + 1])
                last.then_inc(exp_done, 1)

            def take_probT(j):
                act.wait_ge(t_done, j + 1)
                nc.scalar.copy(probT[j % 2][0], bank[4 + 2 * (j % 2)][:, 0:PW]).then_inc(pt_act, 1)

            def take_o(j):
                act.wait_ge(o_done, j + 1)
                if j >= LATE:
                    A(sq[:, j % FOX_PAIRS, :], bank[O_BANK][:, 0:SEQ], ACT.Square)
                    A(oT[:, j, :], bank[O_BANK][:, 0:SEQ], ACT.Copy, scale=gcol[:, KD + j:KD + j + 1]).then_inc(o_taken, 1)
                else:
                    nc.scalar.copy(oT[:, j, :], bank[O_BANK][:, 0:SEQ]).then_inc(o_taken, 1)

            exps(0)
            exps(1)
            take_v(5)
            split_hi(7)
            act.wait_ge(w_lo_ready, 6)
            take_mqk(6)
            split_hi(8)
            take_probT(0)
            take_probT(1)
            take_mqk(7)
            split_hi(9)
            take_o(0)
            take_o(1)
            exps(2)
            exps(3)
            take_mqk(8)
            split_hi(10)
            take_mqk(9)
            split_hi(11)
            take_probT(2)
            take_probT(3)
            take_v(10)
            take_o(2)
            take_o(3)
            act.wait_ge(xt_done, 1)
            for i in range(2):
                last = nc.scalar.copy(qT[:, 4 + 2 * i:6 + 2 * i, :].rearrange("p a b -> p (a b)"), bank[4 + i][:, :])
            last.then_inc(xt_act, 1)
            exps(4)
            exps(5)
            take_v(11)
            seed_rsqrt(2)
            take_probT(4)
            take_probT(5)
            take_o(4)
            take_o(5)
            act.dma_start(gffn, I["norm_ffn_g"].to_broadcast([P, D])).then_inc(gffn_in, 16)
            act.wait_ge(pad_clear, 1)
            act.dma_start(wr[:, :, 0:N_GROUPS], I["w_router_group"][0].rearrange("(k p) g -> p k g", p=P)).then_inc(wr_in, 16)
            act.dma_start(wr[:, :, 8:LG], I["w_router_expert"][0].rearrange("(k p) g e -> p k (g e)", p=P)).then_inc(wr_in, 16)
            exps(6)
            exps(7)
            take_probT(6)
            take_probT(7)
            take_o(6)
            take_o(7)
            act.wait_ge(s_done, PAIRS)
            act.dma_start(biasb[:, 0:N_GROUPS], I["b_router_group"].to_broadcast([P, N_GROUPS])).then_inc(bias_in, 16)
            act.dma_start(biasb[:, 8:LG], I["b_router_expert"].rearrange("o g e -> o (g e)").to_broadcast([P, E])).then_inc(bias_in, 16)
            load_table(ACT.Sqrt)
            seed_rsqrt(3)

            def square_x(t, half):
                act.wait_ge(dve_took, G_OM - G_OF + 2 * t + half + 1)
                ins = A(pp[:, (2 * t + half) * HALF:(2 * t + half + 1) * HALF], x[:, t, half * HALF:(half + 1) * HALF], ACT.Square,
                        accum_out=sq4[:, 2 * t + half:2 * t + half + 1])
                if half == 1:
                    ins.then_inc(ssq_ready, 1)

            def gain_x(t, tiles, b, n):
                act.wait_ge(x2t_done, n + 1)
                for i, k in enumerate(tiles):
                    last = A(h2T[:, k, t * P:(t + 1) * P], bank[b][:, i * P:(i + 1) * P], ACT.Copy, scale=gcol[:, 2 * KD + k:2 * KD + k + 1])
                last.then_inc(h2T_act, 1)

            def take_logits(t):
                act.wait_ge(lgT_done, t + 1)
                nc.scalar.copy(lgT[:, t * P:(t + 1) * P], bank[O_BANK][:, t * P:(t + 1) * P]).then_inc(lgT_ready, 1)

            def high_part(t, c, n):
                act.wait_ge(h2_ready, n)
                nc.scalar.copy(hs[:, 0, t, c, :], h2[:, t, :].rearrange("p (c k) -> p k c", k=KD)[:, c]).then_inc(hi_ready, 1)

            square_x(0, 0)
            square_x(0, 1)
            seed_rsqrt(4, 0, 1)
            act.wait_ge(grp_done, G_MV + 2)
            gain_x(0, range(0, 4), 4, 0)
            act.wait_ge(grp_done, G_OF + 4)
            square_x(1, 0)
            def middle_part(t, c, n):
                act.wait_ge(r1_ready, n)
                nc.scalar.copy(hs[:, 2, t, c, :], res[:, t, c, :]).then_inc(mid_ready, 1)

            high_part(0, slice(0, KD), 1)
            take_logits(0)
            gain_x(1, range(0, 4), 6, 2)
            square_x(1, 1)
            gain_x(1, (6, 7), 4, 4)
            seed_rsqrt(5, 1, 1)
            middle_part(0, slice(0, KD), 1)
            high_part(1, half_k[0], 2)
            take_logits(1)
            high_part(1, half_k[1], 3)
            load_table(ACT.Exp)
            for n in range(2):
                middle_part(1, half_k[n], 2 + n)
            act.wait_ge(gm_ready, 1)
            for t in range(NT):
                last = A(gexp[:, t, :], lg[:, t, 0:8], ACT.Exp, bias=neg_gtop[:, t:t + 1], accum_out=gsum[:, t:t + 1])
            last.then_inc(gexp_done, 1)
            act.wait_ge(ed_ready, 1)
            for t in range(NT):
                last = A(eratio[:, t:t + 1], etop8[:, t, 1:2], ACT.Exp, bias=neg_etop[:, t:t + 1])
            last.then_inc(eexp_done, 1)

            load_table(ACT.Sigmoid)
            act.wait_ge(split_ready, 2)
            act.dma_start(gfin, I["norm_final_g"].rearrange("(o d) -> o d", o=1).to_broadcast([P, D])).then_inc(gfin_in, 16)

            def one_pass(i):
                act.wait_ge(gu_done, i + 1)
                A(sig, p_gu[:, 0:P], ACT.Sigmoid).then_inc(sig_ready, 1)
                act.wait_ge(actt_done, i + 1)
                nc.scalar.copy(actT, p_tr[:, 2 * P:3 * P]).then_inc(actT_ready, 1)
                nc.scalar.copy(wcol, p_tr[:, 3 * P:3 * P + 1]).then_inc(wcol_ready, 1)
                act.wait_ge(added, i + 1)
                nc.scalar.copy(selT[:, :], p_tr[:, 0:SEQ]).then_inc(selT_ready, 1)
                act.wait_ge(wcol_ready, i + 1)
                act.wait_ge(down_done, i + 1)
                for half in range(2):
                    rows = slice(CP * half, CP * (half + 1))
                    A(yb[half][rows, :], p_y[rows, :], ACT.Copy, scale=wcol[rows, :]).then_inc(y_hi_ready, 1)

            act.wait_ge(base_ready, 1)
            passes_all = act.value_load(base[0:1, COUPLES:COUPLES + 1], min_val=COUPLES, max_val=ITEMS_MAX)
            with act.Fori(0, passes_all) as i:
                one_pass(i)
            load_table(ACT.Sqrt)
            for t, half in ((0, 0), (0, 1), (1, 1)):
                act.wait_ge(acc_done, NT * half + t + 1)
                last = A(outb[t][:, half * HALF:(half + 1) * HALF], acc[t][half][:, :], ACT.Square,
                         accum_out=ssq4[:, t, half:half + 1])
            last.then_inc(ssq_ready, 1)
            seed_rsqrt(6)
            act.wait_ge(rstd_ready, 1)
            A(outb[1][:, HALF:D], acc[1][1][:, :], ACT.Copy, scale=rstd[:, 1:2]).then_inc(scaled, 1)

        @block.gpsimd
        def _(pool):
            steps = [0]

            def step(ins):
                steps[0] += 1
                ins.then_inc(pool_step, 1)
                pool.wait_ge(pool_step, steps[0])

            def rotate(g):
                w, c = (g - G_MQ) // 2, (g % 2) * UNIT
                pool.wait_ge(act_took, g + 1)
                heads = mqk[:, w, :, c:c + UNIT].rearrange("p t (h c) -> p t h c", c=HD)
                t1, t2 = heads[:, :, :, 0:ROT], heads[:, :, :, ROT:2 * ROT]
                cos, sin = (cf[:, c:c + NT * ROT].rearrange("p (t r) -> p t r", t=NT).unsqueeze(2).to_broadcast([P, NT, N_MOBA // 2, ROT])
                            for c in (C_COS, C_SIN))
                for i, (a, b) in enumerate(((t1, cos), (t2, sin), (t2, cos), (t1, sin))):
                    last = nc.gpsimd.tensor_tensor(ropet[:, i], a, b, ALU.mult)
                step(last)
                nc.gpsimd.tensor_tensor(t1, ropet[:, 0], ropet[:, 1], ALU.subtract)
                last = nc.gpsimd.tensor_tensor(t2, ropet[:, 2], ropet[:, 3], ALU.add)
                step(last)
                pool.sem_inc(rope_done, 1)

            def square_and_scale(j):
                n = j % FOX_PAIRS
                pool.wait_ge(o_taken, j + 1)
                if j == FOX_PAIRS:
                    pool.wait_ge(ss_done, 1)
                if j < LATE:
                    step(nc.gpsimd.tensor_tensor(sq[:, n, :], oT[:, j, :], oT[:, j, :], ALU.mult))
                    nc.gpsimd.tensor_scalar(oT[:, j, :], oT[:, j, :], gcol[:, KD + j:KD + j + 1], None, ALU.mult).then_inc(o_ready, 1)
                if n > 0:
                    step(nc.gpsimd.tensor_tensor(sq[:, 0, :], sq[:, 0, :], sq[:, n, :], ALU.add))
                if n == FOX_PAIRS - 1:
                    pool.sem_inc(sq_ready, 1)

            k = slice(0, KD // 2)
            pool.wait_ge(w_hi_ready, 1)
            nc.gpsimd.tensor_tensor(unit_lo[0][:, k, :], unit_src(0)[:, k, :], unit_hi[0][:, k, :].bitcast(fp32),
                                    ALU.subtract).then_inc(half_lo_ready, 1)
            pool.wait_ge(cst_in, 16)
            pool.wait_ge(gcol_set, 1)
            rotate(G_MQ)
            rotate(G_MQ + 1)
            square_and_scale(0)
            square_and_scale(1)
            rotate(G_MK)
            rotate(G_MK + 1)
            for j in range(2, PAIRS):
                square_and_scale(j)
            def rest(t, c):
                nc.gpsimd.tensor_tensor(res[:, t, c, :], h2[:, t, :].rearrange("p (c k) -> p k c", k=KD)[:, c],
                                        hs[:, 0, t, c, :], ALU.subtract).then_inc(r1_ready, 1)

            def low_part(t, c, n):
                pool.wait_ge(mid_ready, n)
                return nc.gpsimd.tensor_tensor(hs[:, 1, t, c, :], res[:, t, c, :], hs[:, 2, t, c, :], ALU.subtract)

            pool.wait_ge(hi_ready, 1)
            rest(0, slice(0, KD))
            pool.wait_ge(grp_done, G_OM + 4)
            low_part(0, slice(0, KD), 1)
            for n in range(2):
                pool.wait_ge(hi_ready, 2 + n)
                rest(1, half_k[n])
            for n in range(2):
                low_part(1, half_k[n], 2 + n).then_inc(split_ready, 1)
            pool.wait_ge(lgT_done, NT)
            nc.gpsimd.memset(selT[:, :].bitcast(fp32), 0.0).then_inc(selT_ready, 1)
            for half in range(2):
                nc.gpsimd.memset(yb[half][:, :].bitcast(fp32), 0.0).then_inc(y_ready, 1)
            pool.wait_ge(gfin_in, 16)
            pool.wait_ge(scaled, 1)
            nc.gpsimd.tensor_tensor(outb[1][:, HALF:D], outb[1][:, HALF:D], gfin[:, HALF:D], ALU.mult).then_inc(pool_fin_ready, 1)

        @block.vector
        def _(dve):
            V = nc.vector
            steps = [0]

            def step(ins):
                steps[0] += 1
                ins.then_inc(dve_step, 1)
                dve.wait_ge(dve_step, steps[0])

            V.memset(onescol, 1.0).then_inc(ones_set, 1)
            V.memset(cpart, 0.0)

            def refine_rsqrt(k, t0=0, n=NT, dst=None):
                c = slice(t0, t0 + n)
                dve.wait_ge(seed_ready, k + 1)
                step(V.reciprocal(seed[:, c], seed[:, c]))
                step(V.scalar_tensor_tensor(out=rt[:, c], in0=seed[:, c], scalar=-0.5, in1=seed[:, c], op0=ALU.mult, op1=ALU.mult))
                step(V.tensor_tensor(rt[:, c], rt[:, c], var[:, c], ALU.mult))
                step(V.scalar_tensor_tensor(out=(rstd if dst is None else dst)[:, c], in0=rt[:, c], scalar=1.5, in1=seed[:, c],
                                            op0=ALU.add, op1=ALU.mult))

            for t in range(NT):
                dve.wait_ge(ssq_ready, t + 1)
                V.tensor_scalar(var[:, t:t + 1], ssq[:, t:t + 1], 1.0 / D, EPS, ALU.mult, ALU.add).then_inc(var_ready, 1)
                refine_rsqrt(t, t, 1)
                V.tensor_scalar(xn[:, t, :], x[:, t, :], rstd[:, t:t + 1], None, ALU.mult).then_inc(xn_ready, 1)
            dve.wait_ge(gcol_set, 1)
            for k in range(KD):
                dve.wait_ge(h_hi_ready, 2 * (k // 2) + 2)
                V.scalar_tensor_tensor(out=h_lo[:, k, :], in0=bank[4 + k // 2][:, (k % 2) * SEQ:(k % 2 + 1) * SEQ], scalar=gcol[:, k:k + 1],
                                       in1=h_hi[:, k, :].bitcast(fp32), op0=ALU.mult, op1=ALU.subtract).then_inc(h_lo_ready, 1)

            def split_lo(u):
                dve.wait_ge(w_hi_ready, u + 1)
                b = unit_buf(u)
                k = slice(KD // 2 if u == 0 else 0, KD)
                V.tensor_tensor(unit_lo[b][:, k, :], unit_src(u)[:, k, :], unit_hi[b][:, k, :].bitcast(fp32), ALU.subtract).then_inc(w_lo_ready, 1)

            split_lo(0)
            split_lo(1)
            dve.wait_ge(wf_hi_ready, 1)
            V.tensor_tensor(wf_lo[:, :, :], wf, wf_hi[:, :, :].bitcast(fp32), ALU.subtract).then_inc(wf_lo_ready, 1)
            split_lo(2)
            split_lo(3)
            split_lo(4)
            dve.wait_ge(fz_ready, 1)
            V.scalar_tensor_tensor(out=fa, in0=fz, scalar=-1.0, in1=fz, op0=ALU.mult, op1=ALU.max).then_inc(fa_ready, 1)
            dve.wait_ge(fl_ready, 1)
            step(V.scalar_tensor_tensor(out=fz, in0=fz, scalar=0.0, in1=fl, op0=ALU.min, op1=ALU.subtract))
            step(V.tensor_tensor_scan(fc, fz, fz, 0.0, ALU.add, ALU.bypass))
            step(V.tensor_copy(cpart[0:N_FOX, :], fc))
            step(V.tensor_tensor(fa, fc, cpart[0:N_FOX, :], ALU.subtract))
            step(V.tensor_copy(cmid, fa))
            V.tensor_copy(cpart[32:32 + N_FOX, :], cmid)
            V.tensor_tensor(cpart[64:64 + N_FOX, :], fa, cmid, ALU.subtract).then_inc(fc_ready, 1)
            split_lo(5)

            def maxima(j):
                dve.wait_ge(s_done, j + 1)
                for h in range(2):
                    for t in range(NT):
                        c, nk = t * P, (t + 1) * P
                        last = V.reduce_max(mx[j % 2][:, 2 * h + t:2 * h + t + 1], bank[4 + 2 * (j % 2) + h][:, c:c + nk], AX)
                step(last)
                V.tensor_scalar(nm[j % 2], mx[j % 2], -SCALE, None, ALU.mult).then_inc(nm_ready, 1)

            def normalise(j):
                dve.wait_ge(exp_done, j + 1)
                step(V.reciprocal(rs[j % 2], rs[j % 2]))
                for h in range(2):
                    for t in range(NT):
                        c, nk = t * P, (t + 1) * P
                        p = prob[j % 2][h][:, c:c + nk]
                        last = V.tensor_scalar(p, p, rs[j % 2][:, 2 * h + t:2 * h + t + 1], None, ALU.mult)
                last.then_inc(p_ready, 1)

            def take_probT(j):
                dve.wait_ge(t_done, j + 1)
                V.tensor_copy(probT[j % 2][1], bank[5 + 2 * (j % 2)][:, 0:PW]).then_inc(pt_dve, 1)

            def add_projection(g, t, half):
                dve.wait_ge(grp_done, g + 1)
                xs = x[:, t, half * HALF:(half + 1) * HALF]
                V.scalar_tensor_tensor(out=xs, in0=grp_bank(g)[:, :], scalar=rstd[:, t:t + 1], in1=xs,
                                       op0=ALU.mult, op1=ALU.add).then_inc(dve_took, 1)

            def group_variance(k):
                dve.wait_ge(ss_done, k)
                V.tensor_scalar(var, bank[O_BANK][:, SEQ:SEQ + NT], 1.0 / FOX_W, EPS, ALU.mult, ALU.add).then_inc(var_ready, 1)

            split_lo(6)
            maxima(0)
            maxima(1)
            normalise(0)
            normalise(1)
            split_lo(7)
            split_lo(8)
            take_probT(0)
            take_probT(1)
            split_lo(9)
            maxima(2)
            maxima(3)
            normalise(2)
            normalise(3)
            split_lo(10)
            split_lo(11)
            take_probT(2)
            take_probT(3)
            dve.wait_ge(xt_done, 1)
            for i in range(2):
                last = V.tensor_copy(kT[:, 4 + 2 * i:6 + 2 * i, :].rearrange("p a b -> p (a b)"), bank[6 + i][:, :])
            last.then_inc(xt_dve, 1)
            maxima(4)
            maxima(5)
            normalise(4)
            normalise(5)
            dve.wait_ge(grp_done, G_OF)
            V.memset(stage[:, D:D + KD * LGP], 0.0).then_inc(pad_clear, 1)
            group_variance(1)
            refine_rsqrt(2)
            add_projection(G_OF, 0, 0)
            take_probT(4)
            take_probT(5)
            maxima(6)
            maxima(7)
            add_projection(G_OF + 1, 0, 1)
            normalise(6)
            normalise(7)
            add_projection(G_OF + 2, 1, 0)
            take_probT(6)
            take_probT(7)
            add_projection(G_OF + 3, 1, 1)
            group_variance(2)
            refine_rsqrt(3)
            dve.wait_ge(dve_took, G_OM - G_OF)
            dve.wait_ge(gffn_in, 16)

            def gain_x(t, tiles, b, n):
                dve.wait_ge(x2t_done, n + 1)
                for i, k in enumerate(tiles):
                    last = V.tensor_scalar(h2T[:, k, t * P:(t + 1) * P], bank[b][:, i * P:(i + 1) * P],
                                           gcol[:, 2 * KD + k:2 * KD + k + 1], None, ALU.mult)
                last.then_inc(h2T_dve, 1)

            def norm_x(t):
                c = slice(t, t + 1)
                dve.wait_ge(ssq_ready, 3 + t)
                step(V.tensor_tensor(var[:, c], sq4[:, 2 * t:2 * t + 1], sq4[:, 2 * t + 1:2 * t + 2], ALU.add))
                V.tensor_scalar(var[:, c], var[:, c], 1.0 / D, EPS, ALU.mult, ALU.add).then_inc(var_ready, 1)
                refine_rsqrt(4 + t, t, 1, rstdf)
                for part in ((slice(0, KD),) if t == 0 else half_k):
                    h, xt, g = (a.rearrange("p (c k) -> p c k", k=KD)[:, :, part] for a in (h2[:, t, :], x[:, t, :], gffn))
                    V.scalar_tensor_tensor(out=h, in0=xt, scalar=rstdf[:, c], in1=g, op0=ALU.mult, op1=ALU.mult).then_inc(h2_ready, 1)

            add_projection(G_OM, 0, 0)
            add_projection(G_OM + 1, 0, 1)
            norm_x(0)
            add_projection(G_OM + 2, 1, 0)
            gain_x(0, range(4, 8), 5, 1)
            add_projection(G_OM + 3, 1, 1)
            gain_x(1, (4, 5), 7, 3)
            norm_x(1)
            dve.wait_ge(bias_in, 32)
            step(V.memset(biasb[:, N_GROUPS:8], NEG))

            dve.wait_ge(logits_done, NT)
            for t in range(NT):
                last = V.scalar_tensor_tensor(out=lg[:, t, :], in0=bank[5][:, t * LGP:t * LGP + LG], scalar=rstdf[:, t:t + 1],
                                              in1=biasb, op0=ALU.mult, op1=ALU.add)
            step(last)
            for t in range(NT):
                last = V.max(top8[:, t, :], lg[:, t, 0:8])
            step(last)
            V.tensor_scalar(neg_gtop, top8[:, :, 0], -1.0, None, ALU.mult).then_inc(gm_ready, 1)
            for t in range(NT):
                last = V.max_index(idx8[:, t, :], top8[:, t, :], lg[:, t, 0:8])
            step(last)
            step(V.tensor_copy(gidx, idx8[:, :, 0]))

            def by_tile(row):
                return row.unsqueeze(1).to_broadcast([P, NT, row.shape[1]])

            step(V.tensor_tensor(gmask, by_tile(iota[:, 0:N_GROUPS]), gidx.unsqueeze(2).to_broadcast([P, NT, N_GROUPS]), ALU.is_equal))
            groups = lg[:, :, 8:LG].rearrange("p t (g e) -> p t g e", g=N_GROUPS)
            step(V.tensor_tensor(emask, groups, gmask.unsqueeze(3).to_broadcast([P, NT, N_GROUPS, EPG]), ALU.mult))
            step(V.tensor_tensor(emask[:, :, 0:2], emask[:, :, 0:2], emask[:, :, 2:4], ALU.add))
            step(V.tensor_tensor(el8, emask[:, :, 0], emask[:, :, 1], ALU.add))
            for t in range(NT):
                last = V.max(etop8[:, t, :], el8[:, t, :])
            step(last)
            V.tensor_scalar(neg_etop, etop8[:, :, 0], -1.0, None, ALU.mult).then_inc(ed_ready, 1)
            for t in range(NT):
                last = V.max_index(eidx8[:, t, :], etop8[:, t, :], el8[:, t, :])
            step(last)
            step(V.tensor_copy(expert, eidx8[:, :, 0:2]))
            step(V.scalar_tensor_tensor(out=expert, in0=gidx.unsqueeze(2).to_broadcast([P, NT, 2]), scalar=float(EPG), in1=expert,
                                        op0=ALU.mult, op1=ALU.add))
            for i, mask in enumerate((is1, is2)):
                last = V.tensor_tensor(mask, by_tile(iota[:, 0:E]), expert[:, :, i:i + 1].to_broadcast([P, NT, E]), ALU.is_equal)
            step(last)
            V.tensor_tensor(member, is1, is2, ALU.add).then_inc(member_ready, 1)
            V.tensor_tensor(memf, is1, is2, ALU.add)
            V.memset(rank[:, :, E:E + 2], -1.0)
            V.memset(wgt[:, :, E:E + 2], 0.0)
            dve.wait_ge(rank_done, 1)
            V.tensor_copy(totals, bank[4][:, 2 * E:3 * E])
            step(V.tensor_scalar(rank[:, :, 0:E], bank[4][:, 0:2 * E].rearrange("p (t e) -> p t e", t=NT), 1.0, None, ALU.add))
            step(V.tensor_tensor(rank[:, :, 0:E], rank[:, :, 0:E], memf, ALU.mult))
            step(V.tensor_scalar(rank[:, :, 0:E], rank[:, :, 0:E], -1.0, None, ALU.add))

            def select(at_e):
                at = rank[:, :, at_e:at_e + 2] if isinstance(at_e, int) else rank[:, :, bass.ds(at_e, 2)]
                for t in range(NT):
                    last = V.tensor_tensor(selb[:, t, :].rearrange("p (e c) -> p e c", e=2),
                                           iota[:, 0:CP].rearrange("p (e c) -> p e c", e=2),
                                           at[:, t, :].unsqueeze(2).to_broadcast([P, 2, CAP]), ALU.is_equal)
                last.then_inc(sel_ready, 1)

            select(0)
            pairs2 = totals.rearrange("p (q e) -> p q e", e=2)
            step(V.tensor_tensor(most, pairs2[:, :, 0], pairs2[:, :, 1], ALU.max))
            step(V.tensor_scalar(passes, most, float(CAP - 1), float(CAP), ALU.add, ALU.max))
            step(V.tensor_scalar(passes, passes, CAP.bit_length() - 1, None, ALU.logical_shift_right))
            V.memset(base[:, 0:1], 0)
            V.tensor_tensor_scan(base[:, 1:COUPLES + 1], passes, passes, 0.0, ALU.add, ALU.bypass).then_inc(base_ready, 1)
            dve.wait_ge(gexp_done, 1)
            dve.wait_ge(eexp_done, 1)
            step(V.scalar_tensor_tensor(out=ew[:, :, 0], in0=eratio, scalar=1.0, in1=gsum, op0=ALU.add, op1=ALU.mult))
            step(V.reciprocal(ew[:, :, 0], ew[:, :, 0]))
            step(V.tensor_tensor(ew[:, :, 1], ew[:, :, 0], eratio, ALU.mult))
            def take_gathered(i):
                dve.wait_ge(gathered, i + 1)
                V.tensor_copy(hg[:, :, :].rearrange("p k c -> p (k c)"), p_hg[:, :]).then_inc(hg_ready, 1)

            take_gathered(0)
            for i, mask in enumerate((is1, is2)):
                last = V.tensor_tensor(mask, mask, ew[:, :, i:i + 1].to_broadcast([P, NT, E]), ALU.mult)
            step(last)
            step(V.tensor_tensor(wgt[:, :, 0:E], is1, is2, ALU.add))

            def weigh(at_e, passes_before):
                dve.wait_ge(sel_ready, passes_before + 1)
                V.tensor_copy(selo.rearrange("p t (h c) -> p t h c", h=2), selb.unsqueeze(2).to_broadcast([P, NT, 2, CP]))
                for t in range(NT):
                    for e in range(2):
                        at, weight = ((a[:, t, at_e + e:at_e + e + 1] if isinstance(at_e, int) else a[:, t, bass.ds(at_e + e, 1)])
                                      for a in (rank, wgt))
                        last = V.tensor_scalar(selw[:, t, :].rearrange("p (h e c) -> p e h c", h=2, e=2)[:, e],
                                               iota[:, 0:CP].rearrange("p (h c) -> p h c", h=2), at, weight,
                                               ALU.is_equal, ALU.mult)
                last.then_inc(selw_ready, 1)

            weigh(0, 0)
            steps0 = steps[0]
            STEPS = 2

            def one_pass(i, after, q):
                dve.wait_ge(selw_ready, i + 1)
                V.tensor_scalar(rank[:, :, bass.ds(2 * q, 2)], rank[:, :, bass.ds(2 * q, 2)], -float(CAP), None,
                                ALU.add).then_inc(dve_step, 1)
                dve.wait_ge(dve_step, i * STEPS + (steps0 + 1))
                at_next = dve.snap(2 * (q + ((i + 1) >= after)))
                select(at_next)
                dve.wait_ge(sig_ready, i + 1)
                V.tensor_tensor(gated, p_gu[:, 0:P], sig, ALU.mult).then_inc(dve_step, 1)
                dve.wait_ge(dve_step, i * STEPS + (steps0 + 2))
                V.tensor_tensor(act_sb, p_gu[:, P:2 * P], gated, ALU.mult).then_inc(act_ready, 1)
                take_gathered(i + 1)
                dve.wait_ge(actt_done, i + 1)
                weigh(at_next, i + 1)
                dve.wait_ge(wcol_ready, i + 1)
                for half in range(2):
                    dve.wait_ge(y_hi_ready, 2 * i + (half + 1))
                    rows, rest = slice(CP * half, CP * (half + 1)), slice(CP * (1 - half), CP * (2 - half))
                    V.scalar_tensor_tensor(out=yb[half][rest, :], in0=p_y[rows, :], scalar=wcol[rows, :],
                                           in1=yb[half][rows, :].bitcast(fp32), op0=ALU.mult, op1=ALU.subtract).then_inc(y_ready, 1)

            def couple(q):
                first = dve.value_load(base[0:1, bass.ds(q, 1)], min_val=0, max_val=ITEMS_MAX)
                after = dve.value_load(base[0:1, bass.ds(q + 1, 1)], min_val=1, max_val=ITEMS_MAX)
                with dve.Fori(first, after) as i:
                    one_pass(i, after, q)

            dve.wait_ge(base_ready, 1)
            with dve.Fori(0, COUPLES) as q:
                couple(q)
            passes_all = dve.value_load(base[0:1, COUPLES:COUPLES + 1], min_val=COUPLES, max_val=ITEMS_MAX)

            dve.wait_ge(gfin_in, 16)

            def own(n):
                dve.wait_ge(dve_step, passes_all * STEPS + (steps0 + n))

            dve.wait_ge(acc_done, 2)
            V.tensor_copy(outb[1][:, 0:HALF], acc[1][0][:, :]).then_inc(dve_step, 1)
            own(1)
            V.scalar_tensor_tensor(out=outb[1][:, 0:HALF], in0=outb[1][:, 0:HALF], scalar=1.0, in1=acc[1][0][:, :],
                                   op0=ALU.mult, op1=ALU.mult, accum_out=ssq4[:, 1, 0:1]).then_inc(dve_step, 1)
            own(2)
            dve.wait_ge(ssq_ready, 5)
            V.tensor_tensor(ssq, ssq4[:, :, 0], ssq4[:, :, 1], ALU.add).then_inc(dve_step, 1)
            own(3)
            V.tensor_scalar(var, ssq, 1.0 / D, EPS, ALU.mult, ALU.add).then_inc(var_ready, 1)
            dve.wait_ge(seed_ready, 7)
            V.reciprocal(seed, seed).then_inc(dve_step, 1)
            own(4)
            V.scalar_tensor_tensor(out=rt, in0=seed, scalar=-0.5, in1=seed, op0=ALU.mult, op1=ALU.mult).then_inc(dve_step, 1)
            own(5)
            V.tensor_tensor(rt, rt, var, ALU.mult).then_inc(dve_step, 1)
            own(6)
            V.scalar_tensor_tensor(out=rstd, in0=rt, scalar=1.5, in1=seed, op0=ALU.add, op1=ALU.mult).then_inc(rstd_ready, 1)
            dve.wait_ge(rstd_ready, 1)
            for t, half in ((0, 0), (0, 1), (1, 0)):
                h = slice(half * HALF, (half + 1) * HALF)
                V.scalar_tensor_tensor(out=outb[t][:, h], in0=acc[t][half][:, :], scalar=rstd[:, t:t + 1], in1=gfin[:, h],
                                       op0=ALU.mult, op1=ALU.mult).then_inc(fin_ready, 1)


_INS = ["x", "norm_mix_g", "w_in", "b_forget", "fox_out_g", "moba_out_g", "w_out", "norm_ffn_g", "w_router_group",
        "b_router_group", "w_router_expert", "b_router_expert", "w_gate", "w_up", "w_down", "norm_final_g"]


def constants(np, bf16):
    half = ROT
    inv = (np.float32(500000.0) ** (-np.arange(half, dtype=np.float32) / np.float32(half))).astype(np.float32)
    ang = np.arange(SEQ, dtype=np.float32)[:, None] * inv[None, :]
    f = np.zeros((P, C_END), np.float32)
    f[:, C_ID:C_ID + P] = np.eye(P)
    f[:, C_IOTA:C_IOTA + P] = np.arange(P) % CAP
    for t in range(NT):
        f[:, C_COS + t * ROT:C_COS + (t + 1) * ROT] = np.cos(ang[t * P:(t + 1) * P])
        f[:, C_SIN + t * ROT:C_SIN + (t + 1) * ROT] = np.sin(ang[t * P:(t + 1) * P])
    b = np.zeros((P, 4 * P), np.float32)
    b[:, 0:P] = np.eye(P)
    b[:, P:2 * P] = np.triu(np.full((P, P), -1e30), 1)
    b[:, 2 * P:3 * P] = np.triu(np.ones((P, P)), 1)
    b[:, 3 * P:4 * P] = 1.0
    n8 = np.zeros((96, N_FOX, P), np.float32)
    for h in range(N_FOX):
        n8[[h, 32 + h, 64 + h], h, :] = -1.0 / SCALE
    a2 = np.zeros((P, LG), np.float32)
    for c in range(LG):
        a2[[c, LGP + c], c] = 1.0
    return {"const_f32": f, "const_bf16": b.astype(bf16), "const_neg8": n8.astype(bf16), "const_add2": a2}


def kernel(**inputs):
    import numpy as np
    import concourse.bacc as bacc
    from concourse.bass_utils import run_bass_kernel_spmd

    nc = bacc.Bacc("TRN2", target_bir_lowering=False, num_devices=1)
    arrays, args = {}, {}
    given = {n: np.ascontiguousarray(inputs[n]) for n in _INS}
    given.update(constants(np, mybir.dt.np(mybir.dt.bfloat16)))
    for name, a in given.items():
        arrays[f"in_{name}_dram"] = a
        args[name] = nc.dram_tensor(f"in_{name}_dram", a.shape, mybir.dt.from_np(a.dtype), kind="ExternalInput").ap()
    out = nc.dram_tensor("out_0_dram", (1, SEQ, D), mybir.dt.float32, kind="ExternalOutput").ap()
    layer_program(nc, args, out)
    r = run_bass_kernel_spmd(nc, [arrays], core_ids=[0])
    return r.results[0]["out_0_dram"]
```
